# Optimizing a Trainium2 kernel written in Bass

```python
import math
import jax, jax.numpy as jnp
from jax import lax
import numpy as np

D_MODEL = 1024
BATCH = 1
SEQ = 512
DEPTH = 2

HEAD_DIM = 64
ROPE_THETA = 500000.0
NORM_EPS = 1e-6
Q_BLOCK = 128
A_HEADS = 4
A_Q_DIM = A_HEADS * 2 * HEAD_DIM
A_K_DIM = A_HEADS * 2 * HEAD_DIM
A_V_DIM = A_HEADS * 2 * HEAD_DIM
B_HEADS = 8
B_Q_DIM = B_HEADS * HEAD_DIM
B_KV_DIM = HEAD_DIM
IDX_HEADS = 4
IDX_DIM = 32
IDX_Q_DIM = IDX_HEADS * IDX_DIM
IDX_TOPK_MAX = 256
C_HEADS = 8
C_DIM = C_HEADS * HEAD_DIM
MOBA_BLOCK = 256
MOBA_TOPK = 3
MOBA_Q_CHUNK = 64
N_BRANCH = 3
BRANCH_WIDTH = 512
GATE_DIM = N_BRANCH * D_MODEL
IN_SPLIT = (A_Q_DIM, A_K_DIM, A_V_DIM,
            B_Q_DIM, B_KV_DIM, B_KV_DIM, IDX_Q_DIM, IDX_DIM, IDX_HEADS,
            C_DIM, C_DIM, C_DIM,
            GATE_DIM)
D_IN = (A_Q_DIM + A_K_DIM + A_V_DIM + B_Q_DIM + 2 * B_KV_DIM + IDX_Q_DIM + IDX_DIM
        + IDX_HEADS + 3 * C_DIM + GATE_DIM)
D_FF = -(-8 * D_MODEL // (3 * 256)) * 256

kernel_name = "hybrid_diff_dsa_moba_gated_block"

def rms_norm(x, g):
    xf = x.astype(jnp.float32)
    y = xf * lax.rsqrt(jnp.mean(xf * xf, axis=-1, keepdims=True) + NORM_EPS)
    return (y * g.astype(jnp.float32)).astype(x.dtype)

def partial_rope(x, positions):
    rot = x.shape[-1] // 4
    half = rot // 2
    inv = jnp.power(ROPE_THETA, -jnp.arange(half, dtype=jnp.float32) * 2.0 / rot)
    ang = positions.astype(jnp.float32)[:, :, None] * inv
    cos = jnp.cos(ang)[:, :, None, :].astype(x.dtype)
    sin = jnp.sin(ang)[:, :, None, :].astype(x.dtype)
    x1, x2, rest = x[..., :half], x[..., half:rot], x[..., rot:]
    return jnp.concatenate([x1 * cos - x2 * sin, x2 * cos + x1 * sin, rest], axis=-1)

def diff_attention(q, k, v, lam, subln_g, lam_init):
    B, S, H, _, d = q.shape
    nq = S // Q_BLOCK
    qb = q.reshape(B, nq, Q_BLOCK, H, 2, d).swapaxes(0, 1)
    kpos = jnp.arange(S)
    scale = d ** -0.5

    def one_block(args):
        i, qi = args
        qpos = i * Q_BLOCK + jnp.arange(Q_BLOCK)
        logits = jnp.einsum('bqhcd,bkhcd->bhcqk', qi, k,
                            preferred_element_type=jnp.float32) * scale
        causal = kpos[None, :] <= qpos[:, None]
        logits = jnp.where(causal, logits, -jnp.inf)
        p = jax.nn.softmax(logits, axis=-1)
        attn = p[:, :, 0] - lam * p[:, :, 1]
        return jnp.einsum('bhqk,bkhe->bqhe', attn.astype(v.dtype), v)

    out = lax.map(one_block, (jnp.arange(nq), qb))
    out = out.swapaxes(0, 1).reshape(B, S, H, 2 * d)
    out = rms_norm(out, subln_g) * (1.0 - lam_init)
    return out.reshape(B, S, H * 2 * d)

def dsa_attention(q, k, v, iq, ik, iw, topk):
    B, S, H, d = q.shape
    nq = S // Q_BLOCK
    kpos = jnp.arange(S)
    scale = d ** -0.5
    gather = jax.vmap(lambda t, i: t[i])
    qb = q.reshape(B, nq, Q_BLOCK, H, d).swapaxes(0, 1)
    iqb = iq.reshape(B, nq, Q_BLOCK, IDX_HEADS, IDX_DIM).swapaxes(0, 1)
    iwb = iw.reshape(B, nq, Q_BLOCK, IDX_HEADS).swapaxes(0, 1)

    def one_block(args):
        i, qi, iqi, iwi = args
        qpos = i * Q_BLOCK + jnp.arange(Q_BLOCK)
        rel = jax.nn.relu(jnp.einsum('bqhe,bke->bqhk', iqi, ik,
                                     preferred_element_type=jnp.float32))
        score = jnp.einsum('bqh,bqhk->bqk', iwi.astype(jnp.float32), rel)
        score = jnp.where((kpos[None, :] <= qpos[:, None])[None], score, -jnp.inf)
        _, idx = lax.top_k(score, topk)
        valid = idx <= qpos[None, :, None]
        k_sel = gather(k, idx)
        v_sel = gather(v, idx)
        logits = jnp.einsum('bqhd,bqkd->bhqk', qi, k_sel,
                            preferred_element_type=jnp.float32) * scale
        logits = jnp.where(valid[:, None], logits, -jnp.inf)
        p = jax.nn.softmax(logits, axis=-1)
        return jnp.einsum('bhqk,bqkd->bqhd', p.astype(v.dtype), v_sel)

    out = lax.map(one_block, (jnp.arange(nq), qb, iqb, iwb))
    return out.swapaxes(0, 1).reshape(B, S, H * d)

def moba_attention(q, k, v):
    B, S, H, d = q.shape
    nb = -(-S // MOBA_BLOCK)
    pad = nb * MOBA_BLOCK - S

    def to_blocks(t):
        t = jnp.pad(t, ((0, 0), (0, pad), (0, 0), (0, 0)))
        return t.reshape(B, nb, MOBA_BLOCK, H, d).transpose(0, 3, 1, 2, 4)

    kb, vb = to_blocks(k), to_blocks(v)
    kmean = jnp.mean(kb.astype(jnp.float32), axis=3)
    ntop = min(MOBA_TOPK, nb - 1)
    nc = S // MOBA_Q_CHUNK
    qc_all = q.reshape(B, nc, MOBA_Q_CHUNK, H, d).swapaxes(0, 1)
    scale = d ** -0.5
    blk_ids = jnp.arange(nb)
    gather = jax.vmap(jax.vmap(lambda t, i: t[i]))

    def one_chunk(args):
        c, qc = args
        qpos = c * MOBA_Q_CHUNK + jnp.arange(MOBA_Q_CHUNK)
        own = (c * MOBA_Q_CHUNK) // MOBA_BLOCK
        k_own = lax.dynamic_index_in_dim(kb, own, axis=2, keepdims=False)
        v_own = lax.dynamic_index_in_dim(vb, own, axis=2, keepdims=False)
        kpos_own = own * MOBA_BLOCK + jnp.arange(MOBA_BLOCK)
        lo = jnp.einsum('bqhd,bhkd->bhqk', qc, k_own,
                        preferred_element_type=jnp.float32) * scale
        lo = jnp.where(kpos_own[None, :] <= qpos[:, None], lo, -jnp.inf)
        if ntop == 0:
            p = jax.nn.softmax(lo, axis=-1)
            return jnp.einsum('bhqk,bhkd->bqhd', p.astype(v.dtype), v_own)
        gate = jnp.einsum('bqhd,bhnd->bhqn', qc.astype(jnp.float32), kmean)
        gate = jnp.where(blk_ids < own, gate, -jnp.inf)
        _, idx = lax.top_k(gate, ntop)
        valid = idx < own
        k_sel = gather(kb, idx)
        v_sel = gather(vb, idx)
        lp = jnp.einsum('bqhd,bhqnkd->bhqnk', qc, k_sel,
                        preferred_element_type=jnp.float32) * scale
        lp = jnp.where(valid[..., None], lp, -jnp.inf)
        lp = lp.reshape(B, H, MOBA_Q_CHUNK, ntop * MOBA_BLOCK)
        p = jax.nn.softmax(jnp.concatenate([lo, lp], axis=-1), axis=-1)
        po = p[..., :MOBA_BLOCK].astype(v.dtype)
        pp = p[..., MOBA_BLOCK:].reshape(B, H, MOBA_Q_CHUNK, ntop, MOBA_BLOCK).astype(v.dtype)
        return (jnp.einsum('bhqk,bhkd->bqhd', po, v_own)
                + jnp.einsum('bhqnk,bhqnkd->bqhd', pp, v_sel))

    out = lax.map(one_chunk, (jnp.arange(nc), qc_all))
    return out.swapaxes(0, 1).reshape(B, S, H * d)

def hybrid_mixer(h, positions, w_in, w_branch, w_out, lq1, lk1, lq2, lk2, subln_g, lam_init):
    B, S, _ = h.shape
    proj = jnp.einsum('bsd,de->bse', h, w_in)
    offsets = [int(o) for o in np.cumsum(IN_SPLIT)[:-1]]
    (a_q, a_k, a_v, b_q, b_k, b_v, i_q, i_k, i_w,
     c_q, c_k, c_v, gates) = jnp.split(proj, offsets, axis=-1)

    a_q = partial_rope(a_q.reshape(B, S, 2 * A_HEADS, HEAD_DIM), positions)
    a_k = partial_rope(a_k.reshape(B, S, 2 * A_HEADS, HEAD_DIM), positions)
    a_q = a_q.reshape(B, S, A_HEADS, 2, HEAD_DIM)
    a_k = a_k.reshape(B, S, A_HEADS, 2, HEAD_DIM)
    a_v = a_v.reshape(B, S, A_HEADS, 2 * HEAD_DIM)
    lam = (jnp.exp(jnp.sum(lq1.astype(jnp.float32) * lk1.astype(jnp.float32)))
           - jnp.exp(jnp.sum(lq2.astype(jnp.float32) * lk2.astype(jnp.float32)))
           + lam_init)
    y_a = diff_attention(a_q, a_k, a_v, lam, subln_g, lam_init)

    topk = min(IDX_TOPK_MAX, S // 4)
    b_q = partial_rope(b_q.reshape(B, S, B_HEADS, HEAD_DIM), positions)
    b_k = partial_rope(b_k.reshape(B, S, 1, HEAD_DIM), positions)[:, :, 0]
    i_q = partial_rope(i_q.reshape(B, S, IDX_HEADS, IDX_DIM), positions)
    i_k = partial_rope(i_k.reshape(B, S, 1, IDX_DIM), positions)[:, :, 0]
    y_b = dsa_attention(b_q, b_k, b_v, i_q, i_k, i_w, topk)

    c_q = partial_rope(c_q.reshape(B, S, C_HEADS, HEAD_DIM), positions)
    c_k = partial_rope(c_k.reshape(B, S, C_HEADS, HEAD_DIM), positions)
    c_v = c_v.reshape(B, S, C_HEADS, HEAD_DIM)
    y_c = moba_attention(c_q, c_k, c_v)

    g = jax.nn.sigmoid(gates.reshape(B, S, N_BRANCH, D_MODEL))
    ys = jnp.stack([y_a, y_b, y_c], axis=2)
    branches = jnp.einsum('bsnw,nwd->bsnd', ys, w_branch)
    merged = jnp.sum(g * branches, axis=2)
    return jnp.einsum('bsd,de->bse', merged, w_out)

def swiglu(h, w_ffn_in, w_ffn_out):
    gu = jnp.einsum('bsd,df->bsf', h, w_ffn_in)
    gt, up = jnp.split(gu, 2, axis=-1)
    return jnp.einsum('bsf,fd->bsd', jax.nn.silu(gt) * up, w_ffn_out)

def setup_inputs(seed: int = 0) -> dict:
    key = jax.random.key(seed)
    ks = jax.random.split(key, 14)
    f32 = jnp.float32
    x = jax.random.normal(ks[0], (BATCH, SEQ, D_MODEL), f32)
    offset = jax.random.randint(ks[1], (BATCH, 1), 0, 1024, dtype=jnp.int32)
    positions = (offset + jnp.arange(SEQ, dtype=jnp.int32)[None, :]).astype(jnp.int32)
    w_in = jax.random.normal(ks[2], (DEPTH, D_MODEL, D_IN), f32) * D_MODEL ** -0.5
    w_branch = jax.random.normal(ks[3], (DEPTH, N_BRANCH, BRANCH_WIDTH, D_MODEL), f32) * BRANCH_WIDTH ** -0.5
    w_out = jax.random.normal(ks[4], (DEPTH, D_MODEL, D_MODEL), f32) * D_MODEL ** -0.5
    lambda_q1 = jax.random.normal(ks[5], (DEPTH, HEAD_DIM), f32) * 0.1
    lambda_k1 = jax.random.normal(ks[6], (DEPTH, HEAD_DIM), f32) * 0.1
    lambda_q2 = jax.random.normal(ks[7], (DEPTH, HEAD_DIM), f32) * 0.1
    lambda_k2 = jax.random.normal(ks[8], (DEPTH, HEAD_DIM), f32) * 0.1
    subln_g = 1.0 + 0.02 * jax.random.normal(ks[9], (DEPTH, 2 * HEAD_DIM), f32)
    norm_g = 1.0 + 0.02 * jax.random.normal(ks[10], (DEPTH, 4, D_MODEL), f32)
    w_ffn_in = jax.random.normal(ks[11], (DEPTH, D_MODEL, 2 * D_FF), f32) * D_MODEL ** -0.5
    w_ffn_out = jax.random.normal(ks[12], (DEPTH, D_FF, D_MODEL), f32) * D_FF ** -0.5
    return {"x": x, "positions": positions, "w_in": w_in, "w_branch": w_branch,
            "w_out": w_out, "lambda_q1": lambda_q1, "lambda_k1": lambda_k1,
            "lambda_q2": lambda_q2, "lambda_k2": lambda_k2, "subln_g": subln_g,
            "norm_g": norm_g, "w_ffn_in": w_ffn_in, "w_ffn_out": w_ffn_out}

def reference(x, positions, w_in, w_branch, w_out, lambda_q1, lambda_k1, lambda_q2,
              lambda_k2, subln_g, norm_g, w_ffn_in, w_ffn_out):
    for l in range(DEPTH):
        lam_init = 0.8 - 0.6 * math.exp(-0.3 * l)
        h = rms_norm(x, norm_g[l, 0])
        m = hybrid_mixer(h, positions, w_in[l], w_branch[l], w_out[l], lambda_q1[l],
                         lambda_k1[l], lambda_q2[l], lambda_k2[l], subln_g[l], lam_init)
        x = x + rms_norm(m, norm_g[l, 1])
        h = rms_norm(x, norm_g[l, 2])
        x = x + rms_norm(swiglu(h, w_ffn_in[l], w_ffn_out[l]), norm_g[l, 3])
    return x


_drawn_inputs = setup_inputs


def setup_inputs(seed=0):
    import zlib

    import numpy as np

    out = dict(_drawn_inputs(seed))
    spreads = {}
    factors = {}
    for name, (base, spread) in spreads.items():
        noise = np.random.default_rng([zlib.crc32(name.encode()), seed]).standard_normal(out[name].shape)
        drawn = base * np.exp(spread * noise) if base else spread * noise
        out[name] = __import__('jax').numpy.asarray(drawn.astype(out[name].dtype))
    for name, factor in factors.items():
        out[name] = (out[name] * factor).astype(out[name].dtype)
    return out
```

```python
import math
from contextlib import ExitStack

import numpy as np

import concourse.bass as bass
from concourse import mybir
from concourse.alu_op_type import AluOpType as ALU

P = 128
DEPTH, SEQ, D = 2, 512, 1024
KD = D // P
NT = SEQ // P
HD = 64
NPAIR = 4
WIDTH = 512
KW = WIDTH // P
FF = 2816
KF = FF // P
TOPK = min(256, SEQ // 4)
EPS = 1e-6
SCALE = HD ** -0.5
GCOLS = 2048
ARENA_KIB = 89
BIG = 1e30
TAKEN = -3e38

G_QKV = (0, 12, 23)
G_GATE = (6, 17, 29)
G_OUT = 35
G_FIN = 39
G_FOUT = 61
NG = 72

T_QKV = (0, 28, 52)
T_GATE = (12, 36, 64)
T_FIN = 80
NTILE = 124
RING = 4

TILES_OF = dict([(g, 2) for b in (0, 2) for g in range(G_QKV[b], G_QKV[b] + 6)]
                + list(zip(range(G_QKV[1], G_QKV[1] + 5), (2, 2, 2, 1, 1)))
                + [(G_GATE[b] + 3 * half + i, (2, 2, 4)[i]) for b in range(3) for half in range(2) for i in range(3)]
                + [(g, 2) for g in range(G_FIN, G_FOUT)])
TILE_DONE, NACC = [], 0
for _g in sorted(TILES_OF):
    for _i in range(TILES_OF[_g]):
        if _i == TILES_OF[_g] - 1:
            TILE_DONE.append(("group", _g))
        else:
            NACC += 1
            TILE_DONE.append(("tile", NACC))
ACC_FIN = TILE_DONE[T_FIN][1]
assert len(TILE_DONE) == NTILE
Y_DONE = ([("tile", m // 2 + 1) if m % 2 == 0 else ("group", G_OUT + m // 2) for m in range(KD)],
          [("tile", KD // 2 + m + 1) if m < KD - 1 else ("group", NG - 1) for m in range(KD)])
NY = KD // 2 + KD - 1

X0 = 16
ROPE_AT = (0, 8, 15)
NROPE = 23
UNITS = NPAIR * NT
NU = 3 * UNITS
NBC = 2 * UNITS

C_INV64, C_SGN64, C_INV32, C_SGN32, NCONST = 0, 1, 2, 3, 4


def lam_init(layer):
    return 0.8 - 0.6 * math.exp(-0.3 * layer)


def two_pi_parts():
    left, parts = 2 * math.pi, []
    for _ in range(3):
        step = 2.0 ** (math.floor(math.log2(left)) - 7)
        parts.append(math.floor(left / step) * step)
        left -= parts[-1]
    return parts + [left]


def trunk(nc, x_in, pos_in, w_in, lam_in, subg_in, g_in, const_in, out):
    f32, f32r, bf16, i32 = mybir.dt.float32, mybir.dt.float32r, mybir.dt.bfloat16, mybir.dt.int32
    ACT = mybir.ActivationFunctionType
    X = mybir.AxisListType.X
    ctx = ExitStack()
    with ctx:
        def sb(name, shape, dt=f32):
            return ctx.enter_context(nc.sbuf_tensor(name, shape, dt))

        def sem(name):
            return ctx.enter_context(nc.semaphore(name))

        x = sb("x", [P, KD, SEQ])
        hhi = sb("hhi", [P, KD, SEQ], f32r)
        hlo = sb("hlo", [P, KD, SEQ], f32r)
        raw = [sb(f"raw{s}", [P, GCOLS]) for s in range(2)]
        whi = [sb(f"whi{s}", [P, GCOLS], f32r) for s in range(2)]
        wlo = [sb(f"wlo{s}", [P, GCOLS], f32r) for s in range(2)]
        cos64, sin64, cos32, sin32 = (sb(n, [P, SEQ]) for n in ("cos64", "sin64", "cos32", "sin32"))
        tmp = [sb(f"tmp{i}", [P, SEQ]) for i in range(3)]
        ident = sb("ident", [P, P])
        identb = sb("identb", [P, P], bf16)
        causal = sb("causal", [P, P])
        causalb = sb("causalb", [P, P], bf16)
        ones = sb("ones", [P, P])
        const = sb("const", [P, NCONST])
        eps = sb("eps", [P, 1])
        g_all = sb("g_all", [P, DEPTH, 4 * KD])
        g_cur = sb("g_cur", [P, 4 * KD])
        subg_all = sb("subg_all", [P, DEPTH, P])
        subg = sb("subg", [P, P])
        lam_s = sb("lam_s", [P, DEPTH, 2])
        neglam_all = sb("neglam_all", [P, DEPTH])
        neglam = sb("neglam", [P, 1])
        negmax = sb("negmax", [P, UNITS, 2])
        esum = sb("esum", [P, UNITS, 2])
        rinv = sb("rinv", [P, UNITS, 2])
        ysq = sb("ysq", [P, UNITS])
        ystd = sb("ystd", [P, UNITS])
        yrs = sb("yrs", [P, UNITS])
        top8 = sb("top8", [P, 8])
        y0 = sb("y0", [P, SEQ])
        unused = sb("unused", [P, P])

        arena_at = -(-nc.sbuf_base // 32) * 32
        sb("arena", [P, ARENA_KIB * 256])
        assert nc.sbuf_base == arena_at + ARENA_KIB * 1024

        def at(name, kib, shape, dt=f32):
            return nc.alloc_sbuf_tensor_at(name, shape, dt, offset=arena_at + kib * 1024)

        lam_v = at("lam_v", 0, [P, DEPTH * 4, HD])
        q = at("q", 0, [P, NPAIR, SEQ])
        k = at("k", 8, [P, NPAIR, SEQ])
        v = at("v", 16, [P, NT, WIDTH])
        iq = at("iq", 24, [P, SEQ])
        ik = at("ik", 26, [P, SEQ])
        bvw = at("bvw", 28, [P, NT, P])
        maskb = at("maskb", 30, [P, NT - 1, SEQ], bf16)
        score = at("score", 33, [P, SEQ])
        term = at("term", 35, [P, SEQ])
        ytok = at("ytok", 37, [P, UNITS, P])
        prob = [at(f"prob{i}", 45 + 4 * i, [P, 2, SEQ]) for i in range(3)]
        pt = [at(f"pt{i}", 57 + 4 * i, [P, 2, NT, P]) for i in range(2)]
        yhi = at("yhi", 45, [P, KW, SEQ], f32r)
        ylo = at("ylo", 53, [P, KW, SEQ], f32r)
        gate = at("gate", 65, [P, RING, SEQ])
        merged = at("merged", 73, [P, KD, SEQ])
        mhi = at("mhi", 0, [P, KD, SEQ], f32r)
        mlo = at("mlo", 16, [P, KD, SEQ], f32r)
        rs = at("rs", 65, [P, SEQ])
        res = [at(f"res{i}", 67 + 2 * i, [P, SEQ]) for i in range(2)]
        ahi = at("ahi", 0, [P, KF, SEQ], f32r)
        alo = at("alo", 44, [P, KF, SEQ], f32r)

        ps = ctx.enter_context(nc.psum_tensor("ps", [P, 8, SEQ], f32))

        small_loaded, stored = sem("small_loaded"), sem("stored")
        consts_made, lam_dots_ready, prelude_exp = sem("consts_made"), sem("lam_dots_ready"), sem("prelude_exp")
        angle_ready, sin_done = sem("angle_ready"), sem("sin_done")
        raw_full = [sem(f"raw_full{s}") for s in range(2)]
        whi_ready = [sem(f"whi_ready{s}") for s in range(2)]
        w_ready = [sem(f"w_ready{s}") for s in range(2)]
        group_done = [sem(f"group_done{s}") for s in range(2)]
        acc_ready = sem("acc_ready")
        acc_free = [sem(f"acc_free{b}") for b in range(RING)]
        sq_ready, sq_used, std_ready = sem("sq_ready"), sem("sq_used"), sem("std_ready")
        pre_ready, hhi_ready, h_ready, x_ready = sem("pre_ready"), sem("hhi_ready"), sem("h_ready"), sem("x_ready")
        y_ready, y0_copied = sem("y_ready"), sem("y0_copied")
        rope_ready = sem("rope_ready")
        idx_ready, idx_used, mask_ready = sem("idx_ready"), sem("idx_used"), sem("mask_ready")
        s_ready, max_ready, exp_ready, diff_ready = sem("s_ready"), sem("max_ready"), sem("exp_ready"), sem("diff_ready")
        t_ready, pt0_ready, pt1_ready = sem("t_ready"), sem("pt0_ready"), sem("pt1_ready")
        o_ready, ytok_ready, ysq_ready, ystd_ready = sem("o_ready"), sem("ytok_ready"), sem("ysq_ready"), sem("ystd_ready")
        ynorm_ready, yt_ready, yhi_ready, y_split = sem("ynorm_ready"), sem("yt_ready"), sem("yhi_ready"), sem("y_split")
        m_split = sem("m_split")
        act_split = sem("act_split")

        def units():
            for u in range(UNITS):
                yield u, u // NT, u % NT, (u % NT + 1) * P

        block = ctx.enter_context(nc.Block())

        @block.sync
        def _(sp):
            sp.dma_start(const[:], const_in).then_inc(small_loaded, 16)
            sp.dma_start(tmp[0][:].bitcast(i32), pos_in.to_broadcast([P, SEQ])).then_inc(small_loaded, 16)
            sp.dma_start(x[:], x_in).then_inc(x_ready, X0)
            sp.dma_start(g_all[:], g_in).then_inc(small_loaded, 16)
            sp.dma_start(subg_all[:].rearrange("p l n -> p (l n)"), subg_in.to_broadcast([P, DEPTH * P])).then_inc(small_loaded, 16)
            sp.dma_start(lam_v[:].rearrange("p l n -> p (l n)"), lam_in.to_broadcast([P, DEPTH * 4 * HD])).then_inc(small_loaded, 16)
            for s in range(2):
                sp.dma_start(raw[s][:], w_in[s]).then_inc(raw_full[s], 16)
            with sp.Fori(1, DEPTH * NG // 2) as j:
                for s in range(2):
                    sp.wait_ge(w_ready[s], j)
                    sp.dma_start(raw[s][:], w_in[bass.ds(j * 2 + s, 1), :, :].rearrange("g p n -> (g p) n")).then_inc(raw_full[s], 16)
            for c in range(KD):
                sp.wait_ge(x_ready, X0 + DEPTH * 2 * KD - KD + c + 1)
                sp.dma_start(out[:, c, :], x[:, c, :]).then_inc(stored, 16)
            sp.wait_ge(stored, 16 * KD)

        @block.gpsimd
        def _(pool):
            for t in (ident, identb, causal, causalb):
                pool.memset(t[:], 0.0).then_inc(consts_made, 1)
            pool.memset(ones[:], 1.0).then_inc(consts_made, 1)
            pool.memset(eps[:], EPS).then_inc(consts_made, 1)
            pool.wait_ge(consts_made, 6)
            for t in (ident, identb):
                pool.affine_select(out=t[:], in_=t[:], compare_op=ALU.not_equal, fill=1.0, base=0,
                                   pattern=[[-1, P]], channel_multiplier=1).then_inc(consts_made, 1)
            for t in (causal, causalb):
                pool.affine_select(out=t[:], in_=t[:], compare_op=ALU.is_ge, fill=-BIG, base=0,
                                   pattern=[[-1, P]], channel_multiplier=1).then_inc(consts_made, 1)
            def split(s, loaded, passed, now):
                if passed is not None:
                    pool.wait_ge(raw_full[s], 16)
                pool.wait_ge(raw_full[s], loaded)
                if passed is not None:
                    pool.wait_ge(group_done[s], passed)
                pool.tensor_copy(whi[s][:], raw[s][:]).then_inc(whi_ready[s], 1)
                pool.wait_ge(whi_ready[s], now)
                pool.tensor_tensor(wlo[s][:], raw[s][:], whi[s][:].bitcast(f32), ALU.subtract).then_inc(w_ready[s], 1)

            for s in range(2):
                split(s, 16, None, 1)
            passed, now = pool.alloc_register("passed"), pool.alloc_register("now")
            pool.reg_mov(passed, 1)
            with pool.Fori(32, 16 * (DEPTH * NG // 2) + 16, 16) as loaded:
                pool.reg_add(now, passed, 1)
                for s in range(2):
                    split(s, loaded, passed, now)
                pool.reg_add(passed, passed, 1)

        @block.tensor
        def _(pe):
            pe.wait_ge(consts_made, 10)

            def group_wait(l, g):
                pe.wait_ge(w_ready[g % 2], l * (NG // 2) + g // 2 + 1)

            def bank_wait(l, t):
                if t >= RING:
                    pe.wait_ge(acc_free[t % RING], l * (NTILE // RING) + t // RING)

            def product(dst, terms, rhs):
                rhi, rlo = rhs
                n = len(terms)
                for i, (wh, wl, c) in enumerate(terms):
                    pe.matmul(dst, wh, rhi(c), start=(i == 0), stop=False)
                    pe.matmul(dst, wh, rlo(c), start=False, stop=False)
                    last = pe.matmul(dst, wl, rhi(c), start=False, stop=(i == n - 1))
                return last

            def cols(s, kk, width, c0, n):
                o = kk * width + c0
                return whi[s][:, o:o + n], wlo[s][:, o:o + n]

            h = (lambda c: hhi[:, c, :], lambda c: hlo[:, c, :])
            y = (lambda c: yhi[:, c, :], lambda c: ylo[:, c, :])
            m_ = (lambda c: mhi[:, c, :], lambda c: mlo[:, c, :])

            def feature_tiles(l, g, t, n=2, nk=KD, width=256, rhs=h):
                group_wait(l, g)
                for i in range(n):
                    bank_wait(l, t + i)
                    last = product(ps[:, (t + i) % RING, :],
                                   [(*cols(g % 2, kk, width, i * P, P), kk) for kk in range(nk)], rhs)
                    last.then_inc(group_done[g % 2] if i == n - 1 else acc_ready, 1)

            def token_tiles(l, g, t, ntile, per, width):
                group_wait(l, g)
                s = g % 2
                for i in range(ntile):
                    bank_wait(l, t + i)
                    for j in range(per):
                        tt = i * per + j
                        dst = ps[:, (t + i) % RING, j * width:(j + 1) * width]
                        for kk in range(KD):
                            hh, hl = (a[:, kk, tt * P:(tt + 1) * P] for a in (hhi, hlo))
                            wh, wl = (a[s][:, kk * 256:kk * 256 + width] for a in (whi, wlo))
                            pe.matmul(dst, hh, wh, start=(kk == 0), stop=False)
                            pe.matmul(dst, hh, wl, start=False, stop=False)
                            last = pe.matmul(dst, hl, wh, start=False, stop=(kk == KD - 1))
                    last.then_inc(group_done[s] if i == ntile - 1 else acc_ready, 1)

            def statistic(l, n):
                for c in range(KD):
                    pe.wait_ge(sq_ready, l * 4 * KD + n * KD + c + 1)
                    if c == 0 and n % 2:
                        pe.wait_ge(y0_copied, l * 2 + n // 2 + 1)
                    pe.matmul(ps[:, 0, :], ones[:], tmp[c % 3][:], start=(c == 0), stop=(c == KD - 1)).then_inc(sq_used, 1)

            def indexer(l):
                pe.wait_ge(rope_ready, l * NROPE + ROPE_AT[2])
                for i in range(1, NT):
                    if i > 1:
                        pe.wait_ge(idx_used, l * (NT - 1) + i - 1)
                    for hh in range(4):
                        r = slice(32 * hh, 32 * hh + 32)
                        mm = pe.matmul(ps[:, 4 + hh, 0:(i + 1) * P], iq[r, i * P:(i + 1) * P], ik[r, 0:(i + 1) * P],
                                       start=True, stop=True)
                    mm.then_inc(idx_ready, 1)

            def logits(l, b, u, p, i, w):
                n = l * NU + b * UNITS + u
                if u >= 2:
                    pe.wait_ge(exp_ready, n - 1)
                if b == 1 and i >= 1 and u < NT:
                    pe.wait_ge(mask_ready, l * (NT - 1) + i)
                for c in range(2):
                    r = slice(HD * c, HD * c + HD)
                    kt = k[r, 0 if b == 1 else p, 0:w]
                    bank = 2 * (u % 2) + c
                    pe.matmul(ps[:, bank, 0:w], q[r, p, i * P:(i + 1) * P], kt, start=True, stop=False)
                    if b == 1 and i >= 1:
                        mm = pe.matmul(ps[:, bank, 0:w], identb[:], maskb[:, i - 1, 0:w], start=False, stop=True)
                    else:
                        mm = pe.matmul(ps[:, bank, i * P:w], identb[:], causalb[:], start=False, stop=True)
                mm.then_inc(s_ready, 1)

            def pt_bank(b, u, c):
                return 4 + (u % 2 if b == 0 else c)

            def transposes(l, b, u, p, i, w):
                n = l * NU + b * UNITS + u
                if b == 0:
                    pe.wait_ge(diff_ready, l * UNITS + u + 1)
                    if u >= 2:
                        pe.wait_ge(pt0_ready, n - 1)
                else:
                    pe.wait_ge(exp_ready, n + 1)
                    if u >= 1:
                        pe.wait_ge(pt0_ready, n)
                        pe.wait_ge(pt1_ready, l * NBC + (b - 1) * UNITS + u)
                for c in range(1 if b == 0 else 2):
                    for kb in range(i + 1):
                        mm = pe.transpose(ps[:, pt_bank(b, u, c), kb * P:(kb + 1) * P],
                                          prob[u % 3][:, c, kb * P:(kb + 1) * P], ident[:])
                mm.then_inc(t_ready, 1)

            def values(l, b, u, p, i, w):
                n = l * NU + b * UNITS + u
                pe.wait_ge(pt0_ready, n + 1)
                if b:
                    pe.wait_ge(pt1_ready, l * NBC + (b - 1) * UNITS + u + 1)
                if u >= 2:
                    pe.wait_ge(ytok_ready, n - 1)
                for c in range(1 if b == 0 else 2):
                    for kb in range(i + 1):
                        vals = (v[:, kb, p * P:(p + 1) * P], bvw[:, kb, 0:HD], v[:, kb, p * P + c * HD:p * P + (c + 1) * HD])[b]
                        dst = ps[:, 6 + u % 2, 0:P] if b == 0 else ps[:, 6 + u % 2, c * HD:(c + 1) * HD]
                        mm = pe.matmul(dst, pt[u % 2][:, c, kb, :], vals, start=(kb == 0), stop=(kb == i))
                mm.then_inc(o_ready, 1)

            def attention(l, b):
                pe.wait_ge(rope_ready, l * NROPE + (ROPE_AT + (NROPE,))[b + 1])
                for bank in range(RING):
                    pe.wait_ge(acc_free[bank], l * (NTILE // RING) + T_GATE[b] // RING)
                every = list(units())
                for n in range(UNITS + 3):
                    if n < UNITS:
                        logits(l, b, *every[n])
                    if 0 <= n - 2 < UNITS:
                        transposes(l, b, *every[n - 2])
                    if 0 <= n - 3:
                        values(l, b, *every[n - 3])

            def to_features(l, b):
                for p in range(NPAIR):
                    if b == 0:
                        pe.wait_ge(ynorm_ready, l * NPAIR + p + 1)
                    else:
                        pe.wait_ge(ytok_ready, l * NU + b * UNITS + (p + 1) * NT)
                    if p >= 2:
                        pe.wait_ge(y_split, l * 3 * NPAIR + b * NPAIR + p - 1)
                    for i in range(NT):
                        mm = pe.transpose(ps[:, 4 + p % 2, i * P:(i + 1) * P], ytok[:, p * NT + i, :], ident[:])
                    mm.then_inc(yt_ready, 1)

            def gates_and_branch(l, b):
                for half in range(2):
                    g, t = G_GATE[b] + 3 * half, T_GATE[b] + 8 * half
                    feature_tiles(l, g, t)
                    feature_tiles(l, g + 1, t + 2)
                    if half == 0:
                        pe.wait_ge(y_split, l * 3 * NPAIR + (b + 1) * NPAIR)
                    feature_tiles(l, g + 2, t + 4, n=4, nk=KW, width=512, rhs=y)

            with pe.Fori(0, DEPTH) as l:
                statistic(l, 0)
                pe.wait_ge(h_ready, l * 2 * KD + KD)
                for b in range(3):
                    g, t = G_QKV[b], T_QKV[b]
                    feature_tiles(l, g, t)
                    feature_tiles(l, g + 1, t + 2)
                    feature_tiles(l, g + 2, t + 4)
                    if b == 1:
                        feature_tiles(l, g + 3, t + 6, n=1)
                        token_tiles(l, g + 4, t + 7, 1, NT, P)
                        indexer(l)
                    else:
                        feature_tiles(l, g + 3, t + 6)
                        token_tiles(l, g + 4, t + 8, 2, 2, 256)
                        token_tiles(l, g + 5, t + 10, 2, 2, 256)
                    attention(l, b)
                    to_features(l, b)
                    gates_and_branch(l, b)
                for bank in range(RING):
                    pe.wait_ge(acc_free[bank], l * (NTILE // RING) + T_FIN // RING)
                pe.wait_ge(m_split, l * KD + KD)
                for g in range(4):
                    group_wait(l, G_OUT + g)
                    s = (G_OUT + g) % 2
                    for i in range(2):
                        last = product(ps[:, 2 * g + i, :], [(*cols(s, kk, 256, i * P, P), kk) for kk in range(KD)], m_)
                        last.then_inc(group_done[s] if i else y_ready, 1)
                statistic(l, 1)
                statistic(l, 2)
                with pe.Fori(0, KF // 2) as j:
                    pe.wait_ge(h_ready, l * 2 * KD + 2 * KD)
                    for i in range(2):
                        g = G_FIN + i
                        s = g % 2
                        pe.wait_ge(w_ready[s], l * (NG // 2) + j + (g // 2 + 1))
                        for a in range(2):
                            bank = (2 * i + a) % RING
                            pe.wait_ge(acc_free[bank], l * (NTILE // RING) + j + T_FIN // RING)
                            last = product(ps[:, bank, :], [(*cols(s, kk, 256, a * P, P), kk) for kk in range(KD)], h)
                            last.then_inc(group_done[s] if a else acc_ready, 1)
                for bank in range(RING):
                    pe.wait_ge(acc_free[bank], l * (NTILE // RING) + NTILE // RING)

                def ffn_out(s, rhs, first, final):
                    for m in range(KD):
                        for kk in range(2):
                            wh, wl = cols(s, kk, D, m * P, P)
                            ah, al = rhs(kk)
                            pe.matmul(ps[:, m, :], wh, ah, start=(first and kk == 0), stop=False, skip_group_check=True)
                            pe.matmul(ps[:, m, :], wh, al, start=False, stop=False, skip_group_check=True)
                            last = pe.matmul(ps[:, m, :], wl, ah, start=False, stop=(final and kk == 1), skip_group_check=True)
                        if m == KD - 1:
                            last.then_inc(group_done[s], 1)
                        elif final:
                            last.then_inc(y_ready, 1)

                def act_static(k0):
                    return lambda kk: (ahi[:, k0 + kk, :], alo[:, k0 + kk, :])

                group_wait(l, G_FOUT)
                pe.wait_ge(act_split, l * KF + KF)
                ffn_out(G_FOUT % 2, act_static(0), True, False)
                with pe.Fori(0, 4) as j:
                    for i in range(2):
                        g = G_FOUT + 1 + i
                        pe.wait_ge(w_ready[g % 2], l * (NG // 2) + j + (g // 2 + 1))
                        ffn_out(g % 2, lambda kk: tuple(a[:, bass.ds(j * 4 + (2 + 2 * i + kk), 1), :].rearrange("p a n -> p (a n)")
                                                        for a in (ahi, alo)), False, False)
                for i in range(2):
                    g = G_FOUT + 9 + i
                    group_wait(l, g)
                    ffn_out(g % 2, act_static(KF - 4 + 2 * i), False, i == 1)
                statistic(l, 3)

        @block.scalar
        def _(act):
            act.wait_ge(consts_made, 10)
            act.wait_ge(lam_dots_ready, 1)
            act.activation(lam_s[:], lam_s[:], ACT.Exp).then_inc(prelude_exp, 1)
            for i, (dst, sgn) in enumerate(((cos64, None), (sin64, C_SGN64), (cos32, None), (sin32, C_SGN32))):
                act.wait_ge(angle_ready, i + 1)
                scale = 1.0 if sgn is None else const[:, sgn:sgn + 1]
                act.activation(dst[:], dst[:], ACT.Sin, scale=scale).then_inc(sin_done, 1)

            def square(l, n, c, src):
                at_ = l * 4 * KD + n * KD + c
                if c >= 3:
                    act.wait_ge(sq_used, at_ - 2)
                act.activation(tmp[c % 3][:], src, ACT.Square).then_inc(sq_ready, 1)

            def deviation(l, n):
                act.wait_ge(sq_used, l * 4 * KD + (n + 1) * KD)
                act.activation(tmp[0][:], ps[:, 0, :], ACT.Sqrt, scale=1.0 / D, bias=eps[:]).then_inc(std_ready, 1)

            def pre_norm(l, n):
                for c in range(KD):
                    act.wait_ge(x_ready, l * 2 * KD + (X0 + (c + 1 if n else 0)))
                    square(l, n, c, x[:, c, :])
                deviation(l, n)
                for c in range(KD):
                    act.wait_ge(pre_ready, l * 2 * KD + (n // 2) * KD + c + 1)
                    act.activation(hhi[:, c, :], tmp[1 + c % 2][:], ACT.Copy).then_inc(hhi_ready, 1)

            def result_norm(l, n):
                for m in range(KD):
                    how, count = Y_DONE[n // 2][m]
                    if how == "group":
                        act.wait_ge(group_done[count % 2], l * (NG // 2) + count // 2 + 1)
                    else:
                        act.wait_ge(y_ready, l * NY + count)
                    square(l, n, m, ps[:, m, :])
                deviation(l, n)

            def tile_wait(l, t):
                how, count = TILE_DONE[t]
                if how == "group":
                    act.wait_ge(group_done[count % 2], l * (NG // 2) + count // 2 + 1)
                else:
                    act.wait_ge(acc_ready, l * NACC + count)

            def exponentials(l, b, u, p, i, w):
                n = l * NU + b * UNITS + u
                act.wait_ge(max_ready, n + 1)
                if u >= 3:
                    act.wait_ge(t_ready, n - 2)
                for c in range(2):
                    e = act.activation(prob[u % 3][:, c, 0:w], ps[:, 2 * (u % 2) + c, 0:w], ACT.Exp,
                                       bias=negmax[:, u, c:c + 1], accum_out=esum[:, u, c:c + 1])
                e.then_inc(exp_ready, 1)

            def copy_transposed(l, b, u, p, i, w):
                n = l * NU + b * UNITS + u
                act.wait_ge(t_ready, n + 1)
                if u >= 2:
                    act.wait_ge(o_ready, n - 1)
                bank = 4 + (u % 2 if b == 0 else 0)
                act.activation(pt[u % 2][:, 0, 0:i + 1, :], ps[:, bank, 0:w].rearrange("p (k q) -> p k q", q=P),
                               ACT.Copy).then_inc(pt0_ready, 1)

            with act.Fori(0, DEPTH) as l:
                pre_norm(l, 0)
                for b in range(3):
                    t = T_QKV[b]
                    if b == 1:
                        tile_wait(l, t + 7)
                        act.activation(bvw[:].rearrange("p t n -> p (t n)"), ps[:, (t + 7) % RING, :], ACT.Copy)\
                           .then_inc(acc_free[(t + 7) % RING], 1)
                    else:
                        for n in range(4):
                            tile_wait(l, t + 8 + n)
                            vg, hf = n // 2, n % 2
                            act.activation(v[:, 2 * hf:2 * hf + 2, vg * 256:(vg + 1) * 256],
                                           ps[:, (t + n) % RING, :].rearrange("p (t n) -> p t n", t=2), ACT.Copy)\
                               .then_inc(acc_free[(t + n) % RING], 1)
                    every = list(units())
                    for n in range(UNITS + 3):
                        if n < UNITS:
                            exponentials(l, b, *every[n])
                        if 0 <= n - 2 < UNITS:
                            copy_transposed(l, b, *every[n - 2])
                        if b == 0 and n >= 3:
                            u = n - 3
                            if u:
                                act.wait_ge(ysq_ready, l * UNITS + u)
                            act.wait_ge(ytok_ready, l * NU + u + 1)
                            act.activation(unused[:], ytok[:, u, :], ACT.Square, accum_out=ysq[:, u:u + 1]).then_inc(ysq_ready, 1)
                    if b == 0:
                        act.wait_ge(ysq_ready, l * UNITS + UNITS)
                        act.activation(ystd[:], ysq[:], ACT.Sqrt, scale=1.0 / (2 * HD), bias=eps[:]).then_inc(ystd_ready, 1)
                    for p in range(NPAIR):
                        act.wait_ge(yt_ready, l * 3 * NPAIR + b * NPAIR + p + 1)
                        act.activation(yhi[:, p, :], ps[:, 4 + p % 2, :], ACT.Copy).then_inc(yhi_ready, 1)
                    for half in range(2):
                        for i in range(4):
                            t = T_GATE[b] + 8 * half + i
                            tile_wait(l, t)
                            act.activation(gate[:, i, :], ps[:, t % RING, :], ACT.Sigmoid)\
                               .then_inc(acc_free[t % RING], 1)
                result_norm(l, 1)
                pre_norm(l, 2)
                with act.Fori(0, KF // 2) as j:
                    for i in range(2):
                        act.wait_ge(acc_ready, l * NACC + j * 2 + (ACC_FIN + i))
                        act.wait_ge(acc_free[2 * i + 1], l * (NTILE // RING) + j + T_FIN // RING)
                        act.activation(tmp[i][:], ps[:, 2 * i, :], ACT.Silu)\
                           .then_inc(acc_free[2 * i], 1)
                result_norm(l, 3)

        @block.vector
        def _(dve):
            parts = two_pi_parts()
            dve.wait_ge(small_loaded, 16 * 5)
            lam4 = lam_v[:].rearrange("p (l v) d -> p l v d", v=4)
            lam_q, lam_k = lam4[:, :, 0:2, :], lam4[:, :, 2:4, :]
            lam_p = tmp[1][:, 0:DEPTH * 2 * HD].rearrange("p (l v d) -> p l v d", l=DEPTH, v=2)
            dve.tensor_tensor(lam_p, lam_q, lam_k, ALU.mult)
            dve.drain()
            dve.tensor_reduce(lam_s[:], lam_p, axis=X, op=ALU.add).then_inc(lam_dots_ready, 1)
            dve.wait_ge(prelude_exp, 1)
            for layer in range(DEPTH):
                dve.tensor_tensor(neglam_all[:, layer:layer + 1], lam_s[:, layer, 1:2], lam_s[:, layer, 0:1], ALU.subtract)
                dve.drain()
                dve.tensor_scalar(neglam_all[:, layer:layer + 1], neglam_all[:, layer:layer + 1], lam_init(layer), None, ALU.subtract)
                dve.tensor_scalar(subg_all[:, layer, :], subg_all[:, layer, :], 1.0 - lam_init(layer), None, ALU.mult)
            dve.tensor_copy(tmp[1][:], tmp[0][:].bitcast(i32))
            dve.drain()
            for dst, inv, turn in ((cos64, C_INV64, 0.25), (sin64, C_INV64, 0.0), (cos32, C_INV32, 0.25), (sin32, C_INV32, 0.0)):
                dve.drain()
                dve.tensor_scalar(tmp[2][:], tmp[1][:], const[:, inv:inv + 1], None, ALU.mult)
                dve.drain()
                magic = 1.5 * 2 ** 23
                dve.tensor_scalar(dst[:], tmp[2][:], 1 / (2 * math.pi), turn, ALU.mult, ALU.add)
                dve.drain()
                dve.tensor_scalar(dst[:], dst[:], magic, None, ALU.add)
                dve.drain()
                dve.tensor_scalar(dst[:], dst[:], magic, None, ALU.subtract)
                dve.drain()
                for part in parts:
                    dve.scalar_tensor_tensor(tmp[2][:], dst[:], -part, tmp[2][:], ALU.mult, ALU.add)
                    dve.drain()
                dve.tensor_scalar(tmp[2][:], tmp[2][:], turn * 2 * math.pi, 3.1415925, ALU.add, ALU.min)
                dve.drain()
                dve.tensor_scalar(dst[:], tmp[2][:], -3.1415925, None, ALU.max).then_inc(angle_ready, 1)
            dve.wait_ge(sin_done, 4)

            swap = {n: [*range(n // 8, n // 4), *range(n // 8), *range(n // 4, 32)] for n in (64, 32)}

            def tile_wait(l, t):
                dve.drain()
                how, count = TILE_DONE[t]
                if how == "group":
                    dve.wait_ge(group_done[count % 2], l * (NG // 2) + count // 2 + 1)
                else:
                    dve.wait_ge(acc_ready, l * NACC + count)

            def rotate(l, t, dst, cos, sin, mask, scale=1.0):
                src = ps[:, t % RING, :]
                tile_wait(l, t)
                dve.scalar_tensor_tensor(tmp[2][:], src, scale, cos[:], ALU.mult, ALU.mult)
                dve.stream_shuffle(tmp[1][:], src, mask).then_inc(acc_free[t % RING], 1)
                dve.drain()
                dve.scalar_tensor_tensor(tmp[1][:], tmp[1][:], scale, sin[:], ALU.mult, ALU.mult)
                dve.drain()
                dve.tensor_tensor(dst, tmp[1][:], tmp[2][:], ALU.add).then_inc(rope_ready, 1)

            def inverse_deviation(l, n):
                dve.drain()
                dve.wait_ge(std_ready, l * 4 + n + 1)
                dve.reciprocal(rs[:], tmp[0][:])
                dve.drain()

            def pre_norm(l, n):
                inverse_deviation(l, n)
                at_ = l * 2 * KD + (n // 2) * KD
                for c in range(KD + 1):
                    if c < KD:
                        if c >= 2:
                            dve.wait_ge(hhi_ready, at_ + c - 1)
                            dve.wait_ge(h_ready, at_ + c - 1)
                        dve.scalar_tensor_tensor(tmp[1 + c % 2][:], x[:, c, :], g_cur[:, n * KD + c:n * KD + c + 1], rs[:],
                                                 ALU.mult, ALU.mult).then_inc(pre_ready, 1)
                    if c >= 1:
                        dve.wait_ge(hhi_ready, at_ + c)
                        dve.wait_ge(pre_ready, at_ + c)
                        dve.tensor_tensor(hlo[:, c - 1, :], tmp[1 + (c - 1) % 2][:], hhi[:, c - 1, :].bitcast(f32),
                                          ALU.subtract).then_inc(h_ready, 1)

            def result_norm(l, n):
                dve.drain()
                dve.wait_ge(sq_ready, l * 4 * KD + n * KD + 1)
                dve.tensor_copy(y0[:], ps[:, 0, :]).then_inc(y0_copied, 1)
                inverse_deviation(l, n)
                for c in range(KD):
                    if c >= 2:
                        dve.wait_ge(x_ready, l * 2 * KD + (X0 + (n // 2) * KD + c - 1))
                    src = y0[:] if c == 0 else ps[:, c, :]
                    dve.scalar_tensor_tensor(res[c % 2][:], src, g_cur[:, n * KD + c:n * KD + c + 1], rs[:],
                                             ALU.mult, ALU.mult)
                    dve.drain()
                    dve.tensor_tensor(x[:, c, :], x[:, c, :], res[c % 2][:], ALU.add).then_inc(x_ready, 1)

            def top_k(l):
                for i in range(1, NT):
                    w = (i + 1) * P
                    iw = bvw[:, i, HD:HD + 4]
                    dve.drain()
                    dve.wait_ge(idx_ready, l * (NT - 1) + i)
                    if i == 1:
                        t = T_GATE[1] - 1
                        dve.wait_ge(acc_free[t % RING], l * (NTILE // RING) + t // RING + 1)
                    for hh in range(4):
                        dst = score if hh == 0 else term
                        op = dve.tensor_scalar(dst[:, 0:w], ps[:, 4 + hh, 0:w], 0.0, iw[:, hh:hh + 1], ALU.max, ALU.mult)
                        if hh == 3:
                            op.then_inc(idx_used, 1)
                        dve.drain()
                        if hh:
                            dve.tensor_tensor(score[:, 0:w], score[:, 0:w], term[:, 0:w], ALU.add)
                            dve.drain()
                    dve.tensor_tensor(score[:, i * P:w], score[:, i * P:w], causal[:], ALU.add)
                    dve.drain()
                    for _ in range(TOPK // 8):
                        dve.max(out=top8[:], in_=score[:, 0:w])
                        dve.drain()
                        dve.match_replace(out=score[:, 0:w], in_to_replace=top8[:], in_values=score[:, 0:w], imm_value=TAKEN)
                        dve.drain()
                    dve.tensor_scalar(maskb[:, i - 1, 0:w], score[:, 0:w], TAKEN / 2, -BIG, ALU.is_gt, ALU.mult).then_inc(mask_ready, 1)

            def maxima(l, b, u, p, i, w):
                dve.drain()
                dve.wait_ge(s_ready, l * NU + b * UNITS + u + 1)
                s0 = 2 * (u % 2)
                dve.tensor_reduce(negmax[:, u, :], ps[:, s0:s0 + 2, 0:w], axis=X, op=ALU.max, negate=True).then_inc(max_ready, 1)

            def after_exp(l, b, u, p, i, w):
                dve.drain()
                dve.wait_ge(exp_ready, l * NU + b * UNITS + u + 1)
                dve.reciprocal(rinv[:, u, :], esum[:, u, :])
                if b == 0:
                    pr = prob[u % 3]
                    dve.drain()
                    dve.tensor_tensor(rinv[:, u, 1:2], rinv[:, u, 1:2], neglam[:], ALU.mult)
                    dve.tensor_scalar(pr[:, 0, 0:w], pr[:, 0, 0:w], rinv[:, u, 0:1], None, ALU.mult)
                    dve.drain()
                    dve.scalar_tensor_tensor(pr[:, 0, 0:w], pr[:, 1, 0:w], rinv[:, u, 1:2], pr[:, 0, 0:w],
                                             ALU.mult, ALU.add).then_inc(diff_ready, 1)

            def copy_transposed(l, b, u, p, i, w):
                n = l * NU + b * UNITS + u
                dve.wait_ge(t_ready, n + 1)
                if u >= 2:
                    dve.wait_ge(o_ready, n - 1)
                dve.tensor_copy(pt[u % 2][:, 1, 0:i + 1, :], ps[:, 5, 0:w].rearrange("p (k q) -> p k q", q=P)).then_inc(pt1_ready, 1)

            def results(l, b, u, p, i, w):
                dve.wait_ge(o_ready, l * NU + b * UNITS + u + 1)
                o = ps[:, 6 + u % 2, :]
                if b == 0:
                    op = dve.tensor_copy(ytok[:, u, :], o[:, 0:P])
                else:
                    for c in range(2):
                        op = dve.tensor_scalar(ytok[:, u, c * HD:(c + 1) * HD], o[:, c * HD:(c + 1) * HD],
                                               rinv[:, u, c:c + 1], None, ALU.mult)
                op.then_inc(ytok_ready, 1)

            with dve.Fori(0, DEPTH) as l:
                dve.drain()
                dve.tensor_copy(g_cur[:], g_all[:, bass.ds(l, 1), :].rearrange("p a n -> p (a n)"))
                dve.tensor_copy(subg[:], subg_all[:, bass.ds(l, 1), :].rearrange("p a n -> p (a n)"))
                dve.tensor_copy(neglam[:], neglam_all[:, bass.ds(l, 1)])
                dve.drain()
                pre_norm(l, 0)
                for b in range(3):
                    t = T_QKV[b]
                    for i in range(4):
                        rotate(l, t + i, q[:, i, :], cos64, sin64, swap[64], SCALE)
                    if b == 1:
                        rotate(l, t + 4, k[:, 0, :], cos64, sin64, swap[64])
                        rotate(l, t + 5, ik[:], cos32, sin32, swap[32])
                        rotate(l, t + 6, iq[:], cos32, sin32, swap[32])
                        top_k(l)
                    else:
                        for i in range(4):
                            rotate(l, t + 4 + i, k[:, i, :], cos64, sin64, swap[64])
                    every = list(units())
                    for n in range(UNITS + 3):
                        if n < UNITS:
                            maxima(l, b, *every[n])
                        if 1 <= n <= UNITS:
                            after_exp(l, b, *every[n - 1])
                        if b and 0 <= n - 2 < UNITS:
                            copy_transposed(l, b, *every[n - 2])
                        if n >= 3:
                            results(l, b, *every[n - 3])
                    if b == 0:
                        dve.wait_ge(ystd_ready, l + 1)
                        dve.reciprocal(yrs[:], ystd[:])
                        dve.drain()
                        for u, p, i, w in units():
                            op = dve.scalar_tensor_tensor(ytok[:, u, :], ytok[:, u, :], yrs[:, u:u + 1], subg[:], ALU.mult, ALU.mult)
                            if i == NT - 1:
                                op.then_inc(ynorm_ready, 1)
                    for p in range(NPAIR):
                        dve.wait_ge(yhi_ready, l * 3 * NPAIR + b * NPAIR + p + 1)
                        dve.tensor_tensor(ylo[:, p, :], ps[:, 4 + p % 2, :], yhi[:, p, :].bitcast(f32), ALU.subtract).then_inc(y_split, 1)
                    for m in range(KD):
                        t = T_GATE[b] + 8 * (m // 4) + 4 + m % 4
                        tile_wait(l, t)
                        dve.wait_ge(acc_free[t % RING], l * (NTILE // RING) + t // RING)
                        dst = merged[:, m, :] if b == 0 else tmp[1][:]
                        dve.tensor_tensor(dst, ps[:, t % RING, :], gate[:, m % 4, :], ALU.mult)\
                           .then_inc(acc_free[t % RING], 1)
                        if b:
                            dve.drain()
                            dve.tensor_tensor(merged[:, m, :], merged[:, m, :], tmp[1][:], ALU.add)
                        if b == 2:
                            dve.drain()
                            dve.tensor_copy(mhi[:, m, :], merged[:, m, :])
                            dve.drain()
                            dve.tensor_tensor(mlo[:, m, :], merged[:, m, :], mhi[:, m, :].bitcast(f32), ALU.subtract).then_inc(m_split, 1)
                result_norm(l, 1)
                pre_norm(l, 2)
                with dve.Fori(0, KF // 2) as j:
                    for i in range(2):
                        dve.drain()
                        dve.wait_ge(group_done[(G_FIN + i) % 2], l * (NG // 2) + j + ((G_FIN + i) // 2 + 1))
                        dve.wait_ge(acc_free[2 * i], l * (NTILE // RING) + j + (T_FIN // RING + 1))
                        f = bass.ds(j * 2 + i, 1)
                        ah, al = (a[:, f, :].rearrange("p a n -> p (a n)") for a in (ahi, alo))
                        dve.tensor_tensor(tmp[2][:], tmp[i][:], ps[:, 2 * i + 1, :], ALU.mult).then_inc(acc_free[2 * i + 1], 1)
                        dve.drain()
                        dve.tensor_copy(ah, tmp[2][:])
                        dve.drain()
                        dve.tensor_tensor(al, tmp[2][:], ah.bitcast(f32), ALU.subtract).then_inc(act_split, 1)
                result_norm(l, 3)


def groups(a, width):
    kk = GCOLS // width
    kdim, n = a.shape
    a = a.reshape(kdim // (P * kk), kk, P, n // width, width)
    return a.transpose(3, 0, 2, 1, 4).reshape(-1, P, GCOLS)


def weight_stream(w_in, w_branch, w_out, w_ffn_in, w_ffn_out):
    stream = []
    for layer in range(DEPTH):
        w = w_in[layer]
        cut = np.cumsum([0, 512, 512, 512, 512, HD, HD, 128, 32, 4, 512, 512, 512])
        aq, ak, av, bq, bk, bv, iq, ik, iw, cq, ck, cv = (w[:, cut[i]:cut[i] + n] for i, n in enumerate(
            (512, 512, 512, 512, HD, HD, 128, 32, 4, 512, 512, 512)))
        misc = [bk, bk, ik, ik, ik, ik, iq, iq] + ([bv] + [iw] * 16) * 2
        qkv = ([aq, ak, av], [bq] + misc, [cq, ck, cv])
        for b in range(3):
            stream.append(groups(np.concatenate(qkv[b], axis=1), 256))
            gates = groups(w[:, cut[-1] + b * D:cut[-1] + (b + 1) * D], 256)
            branch = groups(w_branch[layer, b], 512)
            for half in range(2):
                stream += [gates[2 * half:2 * half + 2], branch[half:half + 1]]
        stream.append(groups(w_out[layer], 256))
        fin = w_ffn_in[layer].reshape(D, 2, KF, P).transpose(0, 2, 1, 3).reshape(D, 2 * FF)
        stream += [groups(fin, 256), groups(w_ffn_out[layer], D)]
    return np.ascontiguousarray(np.concatenate(stream))


def constants():
    c = np.zeros((P, NCONST), np.float32)
    for n, inv, sgn in ((64, C_INV64, C_SGN64), (32, C_INV32, C_SGN32)):
        rot = n // 4
        freq = np.power(np.float32(500000.0), -np.arange(rot // 2, dtype=np.float32) * np.float32(2.0) / np.float32(rot))
        for p in range(P):
            if p % n < rot:
                c[p, inv] = freq[p % n % (rot // 2)]
                c[p, sgn] = -1.0 if p % n < rot // 2 else 1.0
    return c


def kernel(x, positions, w_in, w_branch, w_out, lambda_q1, lambda_k1, lambda_q2, lambda_k2, subln_g, norm_g,
           w_ffn_in, w_ffn_out):
    import concourse.bacc as bacc
    from concourse.bass_utils import run_bass_kernel_spmd

    x, w_in, w_branch, w_out, w_ffn_in, w_ffn_out = map(np.asarray, (x, w_in, w_branch, w_out, w_ffn_in, w_ffn_out))
    lam = np.stack([np.asarray(a) for a in (lambda_q1, lambda_q2, lambda_k1, lambda_k2)], axis=1)
    arrays = {
        "x_in": np.ascontiguousarray(x[0].T.reshape(KD, P, SEQ).transpose(1, 0, 2)),
        "pos_in": np.ascontiguousarray(np.asarray(positions)),
        "w_in": weight_stream(w_in, w_branch, w_out, w_ffn_in, w_ffn_out),
        "lam_in": np.ascontiguousarray(lam.reshape(1, -1)),
        "subg_in": np.ascontiguousarray(np.asarray(subln_g).reshape(1, -1)),
        "g_in": np.ascontiguousarray(np.asarray(norm_g).reshape(DEPTH, 4 * KD, P).transpose(2, 0, 1)),
        "const_in": constants(),
    }
    nc = bacc.Bacc("TRN2", target_bir_lowering=False, num_devices=1)
    args = [nc.dram_tensor(n, a.shape, mybir.dt.from_np(a.dtype), kind="ExternalInput").ap() for n, a in arrays.items()]
    out = nc.dram_tensor("out", (P, KD, SEQ), mybir.dt.float32, kind="ExternalOutput").ap()
    trunk(nc, *args, out)
    r = run_bass_kernel_spmd(nc, [arrays], core_ids=[0])
    got = np.asarray(r.results[0]["out"])
    return np.ascontiguousarray(got.transpose(1, 0, 2).reshape(D, SEQ).T)[None]
```

```python
import math
from contextlib import ExitStack

import numpy as np

import concourse.bass as bass
from concourse import mybir
from concourse.alu_op_type import AluOpType as ALU

P = 128
DEPTH, SEQ, D = 2, 512, 1024
KD = D // P
NT = SEQ // P
HD = 64
NPAIR = 4
WIDTH = 512
KW = WIDTH // P
FF = 2816
KF = FF // P
TOPK = min(256, SEQ // 4)
EPS = 1e-6
SCALE = HD ** -0.5
GCOLS = 2048
ARENA_KIB = 96
BIG = 1e30
TAKEN = -3e38

G_MISC = 0
G_QKV = (3, 13, 21)
G_GATE = (9, 17, 29)
G_BRANCH = (15, 27, 33)
G_OUT = 35
G_FIN = 39
G_FOUT = 61
NG = 72

T_MISC = 0
T_QKV = (4, 16, 28)
T_BRANCH = (20, 40, 48)
T_ATTENTION = (16, 28, 48)
T_FIN = 56
NTILE = 100
RING = 4
GATE_BANK = 3
NSUM = KD - 1
STAT_BANK = (4, 0)
SRING = 3

TILES_OF = dict([(0, 2), (1, 1), (2, 1)]
                + [(g, 2) for b, n in enumerate((6, 2, 6)) for g in range(G_QKV[b], G_QKV[b] + n)]
                + [(g, 4) for b in range(3) for g in (G_BRANCH[b], G_BRANCH[b] + 1)]
                + [(g, 2) for g in range(G_FIN, G_FOUT)])
TILE_DONE, NACC = [], 0
for _g in sorted(TILES_OF):
    for _i in range(TILES_OF[_g]):
        if _i == TILES_OF[_g] - 1:
            TILE_DONE.append(("group", _g))
        else:
            NACC += 1
            TILE_DONE.append(("tile", NACC))
ACC_FIN = TILE_DONE[T_FIN][1]
assert len(TILE_DONE) == NTILE
Y_DONE = ([("tile", m // 2 + 1) if m % 2 == 0 else ("group", G_OUT + m // 2) for m in range(KD)],
          [("tile", KD // 2 + m + 1) if m < KD - 1 else ("group", NG - 1) for m in range(KD)])
NY = KD // 2 + KD - 1

X0 = KD
ROPE_AT = (11, 15, 23)
NROPE = 23
NIDX = 3
UNITS = NPAIR * NT
NU = 3 * UNITS
MAPS = 2 * UNITS
NM = 3 * MAPS
ROUNDS = TOPK // 8
WMASK = [0, 2 * P, 5 * P, 9 * P]
NBC = 2 * UNITS
ITERATIONS = UNITS + 2
GATE_SPANS = (2, 2, 2, 2, 2, 2, 3, 3)
GATE_STEPS = [m * KD + KD * n // span for m, span in enumerate(GATE_SPANS) for n in range(span)] + [KD * KD]
assert len(GATE_STEPS) == ITERATIONS + 1

C_INV, C_SGN64, C_SGN32, NCONST = 0, 1, 2, 3


def lam_init(layer):
    return 0.8 - 0.6 * math.exp(-0.3 * layer)


def two_pi_parts():
    left, parts = 2 * math.pi, []
    for _ in range(3):
        step = 2.0 ** (math.floor(math.log2(left)) - 7)
        parts.append(math.floor(left / step) * step)
        left -= parts[-1]
    return parts + [left]


def trunk(nc, x_in, pos_in, w_in, lam_in, subg_in, g_in, const_in, out):
    f32, f32r, bf16, i32 = mybir.dt.float32, mybir.dt.float32r, mybir.dt.bfloat16, mybir.dt.int32
    ACT = mybir.ActivationFunctionType
    X = mybir.AxisListType.X
    ctx = ExitStack()
    with ctx:
        def sb(name, shape, dt=f32):
            return ctx.enter_context(nc.sbuf_tensor(name, shape, dt))

        def sem(name):
            return ctx.enter_context(nc.semaphore(name))

        x = sb("x", [P, KD, SEQ])
        hhi = sb("hhi", [P, KD, SEQ], f32r)
        hlo = sb("hlo", [P, KD, SEQ], f32r)
        raw = [sb(f"raw{s}", [P, GCOLS]) for s in range(2)]
        whi = [sb(f"whi{s}", [P, GCOLS], f32r) for s in range(2)]
        wlo = [sb(f"wlo{s}", [P, GCOLS], f32r) for s in range(2)]
        cos64, sin64, cos32, sin32 = (sb(n, [P, SEQ]) for n in ("cos64", "sin64", "cos32", "sin32"))
        tmp = [sb(f"tmp{i}", [P, SEQ]) for i in range(3)]
        ident = sb("ident", [P, P])
        identb = sb("identb", [P, P], bf16)
        causal = sb("causal", [P, P])
        causalb = sb("causalb", [P, P], bf16)
        ones = sb("ones", [P, P])
        const = sb("const", [P, NCONST])
        eps = sb("eps", [P, 1])
        half_pi = sb("half_pi", [P, 1])
        g_all = sb("g_all", [P, DEPTH, 4 * KD])
        g_cur = sb("g_cur", [P, 4 * KD])
        subg_all = sb("subg_all", [P, DEPTH, P])
        subg = sb("subg", [P, P])
        lam_s = sb("lam_s", [P, DEPTH, 2])
        neglam_all = sb("neglam_all", [P, DEPTH])
        neglam = sb("neglam", [P, 1])
        negmax = sb("negmax", [P, UNITS, 2])
        esum = sb("esum", [P, UNITS, 2])
        rinv = sb("rinv", [P, UNITS, 2])
        ratio = sb("ratio", [P, 1])
        started = sb("started", [P, 1])
        dev = sb("dev", [P, NT])
        inv = sb("inv", [P, NT])
        ysq = sb("ysq", [P, UNITS])
        ystd = sb("ystd", [P, UNITS])
        yrs = sb("yrs", [P, UNITS])
        top8 = sb("top8", [P, 8])
        kb = sb("kb", [P, SEQ])
        sumsq = kb
        y0 = sb("y0", [P, SEQ])
        unused = sb("unused", [P, P])

        arena_at = -(-nc.sbuf_base // 32) * 32
        sb("arena", [P, ARENA_KIB * 256])
        assert nc.sbuf_base == arena_at + ARENA_KIB * 1024

        def at(name, kib, shape, dt=f32):
            return nc.alloc_sbuf_tensor_at(name, shape, dt, offset=arena_at + kib * 1024)

        lam_v = at("lam_v", 0, [P, DEPTH * 4, HD])
        q = at("q", 0, [P, NPAIR, SEQ])
        k = at("k", 8, [P, NPAIR, SEQ])
        v = at("v", 16, [P, NT, WIDTH])
        iq = at("iq", 24, [P, SEQ])
        ik = at("ik", 26, [P, SEQ])
        bvw = at("bvw", 28, [P, NT, P])
        maskb = at("maskb", 30, [P, WMASK[-1]], bf16)
        scores = at("scores", 33, [P, WMASK[-1]])
        ytok = at("ytok", 38, [P, UNITS, P])
        prob = [at(f"prob{i}", 46 + 4 * i, [P, 2, SEQ]) for i in range(2)]
        pt = [at(f"pt{i}", 54 + 4 * i, [P, 2, NT, P]) for i in range(2)]
        yhi = at("yhi", 46, [P, KW, SEQ], f32r)
        ylo = at("ylo", 54, [P, KW, SEQ], f32r)
        gate = at("gate", 62, [P, KD, SEQ])
        merged = at("merged", 78, [P, KD, SEQ])
        mhi = at("mhi", 0, [P, KD, SEQ], f32r)
        mlo = at("mlo", 16, [P, KD, SEQ], f32r)
        rs_res = at("rs_res", 88, [P, SEQ])
        res = [at(f"res{i}", 90 + 2 * i, [P, SEQ]) for i in range(2)]
        rs_ffn = at("rs_ffn", 94, [P, SEQ])
        ahi = at("ahi", 0, [P, KF, SEQ], f32r)
        alo = at("alo", 44, [P, KF, SEQ], f32r)

        ps = ctx.enter_context(nc.psum_tensor("ps", [P, 8, SEQ], f32))

        x_loaded = sem("x_loaded")
        lam_loaded, angle_loaded, small_loaded, stored = sem("lam_loaded"), sem("angle_loaded"), sem("small_loaded"), sem("stored")
        consts_made, lam_dots_ready, prelude_exp = sem("consts_made"), sem("lam_dots_ready"), sem("prelude_exp")
        angle_ready, sin_done = sem("angle_ready"), sem("sin_done")
        raw_full = [sem(f"raw_full{s}") for s in range(2)]
        whi_ready = [sem(f"whi_ready{s}") for s in range(2)]
        w_ready = [sem(f"w_ready{s}") for s in range(2)]
        group_done = [sem(f"group_done{s}") for s in range(2)]
        acc_ready = sem("acc_ready")
        acc_free = [sem(f"acc_free{b}") for b in range(RING)]
        sq_ready, sum_ready, stat_ready, std_ready = sem("sq_ready"), sem("sum_ready"), sem("stat_ready"), sem("std_ready")
        inv_ready, rs_ready = sem("inv_ready"), sem("rs_ready")
        pre_ready, hhi_ready, h_ready, x_ready = sem("pre_ready"), sem("hhi_ready"), sem("h_ready"), sem("x_ready")
        y_ready, y0_copied = sem("y_ready"), sem("y0_copied")
        rope_ready = sem("rope_ready")
        idx_ready, idx_used, mask_ready = sem("idx_ready"), sem("idx_used"), sem("mask_ready")
        s_ready, max_ready, exp_ready, diff_ready = sem("s_ready"), sem("max_ready"), sem("exp_ready"), sem("diff_ready")
        t_ready, pt0_ready, pt1_ready = sem("t_ready"), sem("pt0_ready"), sem("pt1_ready")
        o_ready, ytok_ready, ysq_ready, ystd_ready = sem("o_ready"), sem("ytok_ready"), sem("ysq_ready"), sem("ystd_ready")
        ynorm_ready, yt_ready, yhi_ready, y_split = sem("ynorm_ready"), sem("yt_ready"), sem("yhi_ready"), sem("y_split")
        m_split = sem("m_split")
        gate_scaled, silu_ready = sem("gate_scaled"), sem("silu_ready")
        act_split = sem("act_split")
        gate_ready, gate_free, sig_ready = sem("gate_ready"), sem("gate_free"), sem("sig_ready")

        def add_squares(eng, l, n, c):
            eng.wait_ge(sq_ready, l * 4 * KD + n * KD + c + 1)
            eng.tensor_tensor(sumsq[:], sumsq[:] if c > 1 else tmp[0][:], tmp[c % 3][:], ALU.add).then_inc(sum_ready, 1)

        def units():
            for u in range(UNITS):
                yield u, u // NT, u % NT, (u % NT + 1) * P

        block = ctx.enter_context(nc.Block())

        @block.sync
        def _(sp):
            sp.dma_start(lam_v[:].rearrange("p l n -> p (l n)"), lam_in.to_broadcast([P, DEPTH * 4 * HD])).then_inc(lam_loaded, 16)
            sp.dma_start(const[:], const_in).then_inc(angle_loaded, 16)
            sp.dma_start(y0[:].bitcast(i32), pos_in.to_broadcast([P, SEQ])).then_inc(angle_loaded, 16)
            sp.dma_start(x[:], x_in).then_inc(x_loaded, 16)
            sp.dma_start(raw[0][:], w_in[0]).then_inc(raw_full[0], 16)
            sp.dma_start(g_all[:], g_in).then_inc(small_loaded, 16)
            sp.dma_start(subg_all[:].rearrange("p l n -> p (l n)"), subg_in.to_broadcast([P, DEPTH * P])).then_inc(small_loaded, 16)
            sp.dma_start(raw[1][:], w_in[1]).then_inc(raw_full[1], 16)
            with sp.Fori(1, DEPTH * NG // 2) as j:
                for s in range(2):
                    sp.wait_ge(w_ready[s], j)
                    sp.dma_start(raw[s][:], w_in[bass.ds(j * 2 + s, 1), :, :].rearrange("g p n -> (g p) n")).then_inc(raw_full[s], 16)
            for c in range(KD):
                sp.wait_ge(x_ready, X0 + DEPTH * 2 * KD - KD + c + 1)
                sp.dma_start(out[:, c, :], x[:, c, :]).then_inc(stored, 16)
            sp.wait_ge(stored, 16 * KD)

        @block.gpsimd
        def _(pool):
            for t in (ident, identb, causal, causalb):
                pool.memset(t[:], 0.0).then_inc(consts_made, 1)
            pool.memset(ones[:], 1.0).then_inc(consts_made, 1)
            pool.memset(eps[:], EPS).then_inc(consts_made, 1)
            pool.memset(half_pi[:], math.pi / 2).then_inc(consts_made, 1)
            pool.wait_ge(consts_made, 7)
            for t in (ident, identb):
                pool.affine_select(out=t[:], in_=t[:], compare_op=ALU.not_equal, fill=1.0, base=0,
                                   pattern=[[-1, P]], channel_multiplier=1).then_inc(consts_made, 1)
            for t in (causal, causalb):
                pool.affine_select(out=t[:], in_=t[:], compare_op=ALU.is_ge, fill=-BIG, base=0,
                                   pattern=[[-1, P]], channel_multiplier=1).then_inc(consts_made, 1)
            pool.wait_ge(x_loaded, 16)
            pool.memset(started[:], 0.0).then_inc(x_ready, X0)

            def low_weights(l, n, s):
                pool.wait_ge(whi_ready[s], l * (NG // 2) + n + 1)
                pool.tensor_tensor(wlo[s][:], raw[s][:], whi[s][:].bitcast(f32), ALU.subtract).then_inc(w_ready[s], 1)

            def sum_squares(l, n, chunks=range(1, KD)):
                for c in chunks:
                    pool.drain()
                    add_squares(pool, l, n, c)

            with pool.Fori(0, DEPTH) as l:
                sum_squares(l, 0)
                low_weights(l, 0, 0)
                low_weights(l, 0, 1)
                with pool.Fori(1, G_FIN // 2 + 1) as n:
                    for s in range(2):
                        low_weights(l, n, s)
                sum_squares(l, 2, range(1, 5))
                low_weights(l, (G_FIN + 1) // 2, 0)
                sum_squares(l, 2, range(5, KD))
                low_weights(l, (G_FIN + 1) // 2, 1)
                with pool.Fori((G_FIN + 1) // 2 + 1, NG // 2) as n:
                    for s in range(2):
                        low_weights(l, n, s)

        @block.tensor
        def _(pe):
            pe.wait_ge(consts_made, 11)

            def group_wait(l, g):
                pe.wait_ge(w_ready[g % 2], l * (NG // 2) + g // 2 + 1)

            def bank_wait(l, t):
                if t >= RING:
                    pe.wait_ge(acc_free[t % RING], l * (NTILE // RING) + t // RING)

            def product(dst, terms, rhs, first=True, final=True):
                rhi, rlo = rhs
                n = len(terms)
                for i, (wh, wl, c) in enumerate(terms):
                    pe.matmul(dst, wh, rhi(c), start=(first and i == 0), stop=False)
                    pe.matmul(dst, wh, rlo(c), start=False, stop=False)
                    last = pe.matmul(dst, wl, rhi(c), start=False, stop=(final and i == n - 1))
                return last

            def cols(s, kk, width, c0, n):
                o = kk * width + c0
                return whi[s][:, o:o + n], wlo[s][:, o:o + n]

            h = (lambda c: hhi[:, c, :], lambda c: hlo[:, c, :])
            y = (lambda c: yhi[:, c, :], lambda c: ylo[:, c, :])
            m_ = (lambda c: mhi[:, c, :], lambda c: mlo[:, c, :])

            def two_tiles_as_ready(s, banks, chunk_ready, before, rhs, first_done, between=None):
                rhi, rlo = rhs
                for c in range(KD):
                    if between:
                        between(c)
                    pe.wait_ge(chunk_ready, before + (c + 1))
                    for a, bank in enumerate(banks):
                        wh, wl = cols(s, c, 256, a * P, P)
                        pe.matmul(ps[:, bank, :], wh, rhi(c), start=(c == 0), stop=False, skip_group_check=True)
                        pe.matmul(ps[:, bank, :], wh, rlo(c), start=False, stop=False, skip_group_check=True)
                        last = pe.matmul(ps[:, bank, :], wl, rhi(c), start=False, stop=(c == KD - 1), skip_group_check=True)
                        if c == KD - 1:
                            last.then_inc(group_done[s] if a else first_done, 1)

            def feature_tiles(l, g, t, n=2, nk=KD, width=256, rhs=h, before_tile=None):
                group_wait(l, g)
                for i in range(n):
                    if before_tile:
                        before_tile(i)
                    bank_wait(l, t + i)
                    last = product(ps[:, (t + i) % RING, :],
                                   [(*cols(g % 2, kk, width, i * P, P), kk) for kk in range(nk)], rhs)
                    last.then_inc(group_done[g % 2] if i == n - 1 else acc_ready, 1)

            def token_tiles(l, g, t, ntile, per, width):
                group_wait(l, g)
                s = g % 2
                for i in range(ntile):
                    bank_wait(l, t + i)
                    for j in range(per):
                        tt = i * per + j
                        dst = ps[:, (t + i) % RING, j * width:(j + 1) * width]
                        for kk in range(KD):
                            hh, hl = (a[:, kk, tt * P:(tt + 1) * P] for a in (hhi, hlo))
                            wh, wl = (a[s][:, kk * 256:kk * 256 + width] for a in (whi, wlo))
                            pe.matmul(dst, hh, wh, start=(kk == 0), stop=False)
                            pe.matmul(dst, hh, wl, start=False, stop=False)
                            last = pe.matmul(dst, hl, wh, start=False, stop=(kk == KD - 1))
                    last.then_inc(group_done[s] if i == ntile - 1 else acc_ready, 1)

            def token_sums(l, n):
                if n % 2:
                    pe.wait_ge(y0_copied, l * 2 + n // 2 + 1)
                pe.wait_ge(sum_ready, l * 4 * NSUM + (n + 1) * NSUM)
                for j in range(NT):
                    mm = pe.matmul(ps[:, STAT_BANK[n % 2], j:j + 1], sumsq[:, j * P:(j + 1) * P], ones[:, 0:1], start=True, stop=True)
                mm.then_inc(stat_ready, 1)

            def spread_inverse(l, n):
                pe.wait_ge(inv_ready, l * 4 + n + 1)
                for j in range(NT):
                    mm = pe.matmul(ps[:, STAT_BANK[n % 2], j * P:(j + 1) * P], inv[:, j:j + 1].to_broadcast([P, P]), ident[:],
                                   start=True, stop=True)
                mm.then_inc(rs_ready, 1)

            def statistic(l, n):
                token_sums(l, n)
                spread_inverse(l, n)

            def indexer(l, i):
                pe.wait_ge(rope_ready, l * NROPE + NIDX)
                if i > 1:
                    pe.wait_ge(idx_used, l * (NT - 1) + i - 1)
                for hh in range(4):
                    r = slice(32 * hh, 32 * hh + 32)
                    mm = pe.matmul(ps[:, 4 + hh, 0:(i + 1) * P], iq[r, i * P:(i + 1) * P], ik[r, 0:(i + 1) * P],
                                   start=True, stop=True)
                mm.then_inc(idx_ready, 1)

            def logits(l, b, u, p, i, w):
                if b == 1 and i >= 1 and u < NT:
                    pe.wait_ge(mask_ready, l * (NT - 1) + i)
                for c in range(2):
                    m = 2 * u + c
                    if m >= SRING:
                        pe.wait_ge(exp_ready, l * NM + (b * MAPS + m - SRING + 1))
                    r = slice(HD * c, HD * c + HD)
                    kt = kb[r, 0:w] if b == 1 else k[r, p, 0:w]
                    bank = m % SRING
                    pe.matmul(ps[:, bank, 0:w], q[r, p, i * P:(i + 1) * P], kt, start=True, stop=False)
                    if b == 1 and i >= 1:
                        mm = pe.matmul(ps[:, bank, 0:w], identb[:], maskb[:, WMASK[i - 1]:WMASK[i]], start=False, stop=True)
                    else:
                        mm = pe.matmul(ps[:, bank, i * P:w], identb[:], causalb[:], start=False, stop=True)
                    mm.then_inc(s_ready, 1)

            def gate_steps(l, b, n):
                for step in range(GATE_STEPS[n], GATE_STEPS[n + 1]):
                    m, kk = step // KD, step % KD
                    g = G_GATE[b] + m // 2
                    if kk == 0 and m % 2 == 0:
                        group_wait(l, g)
                    if kk == 0 and m:
                        pe.wait_ge(gate_free, l * 3 * KD + (b * KD + m))
                    last = product(ps[:, GATE_BANK, :], [(*cols(g % 2, kk, 256, (m % 2) * P, P), kk)], h,
                                   first=kk == 0, final=kk == KD - 1)
                    if kk == KD - 1:
                        last.then_inc(group_done[g % 2] if m % 2 else gate_ready, 1)

            def pt_bank(b, u, c):
                return 4 + (u % 2 if b == 0 else c)

            def transposes(l, b, u, p, i, w):
                n = l * NU + b * UNITS + u
                if b == 0:
                    pe.wait_ge(diff_ready, l * UNITS + u + 1)
                    if u >= 2:
                        pe.wait_ge(pt0_ready, n - 1)
                else:
                    pe.wait_ge(exp_ready, l * NM + (b * MAPS + 2 * u + 2))
                    if u >= 1:
                        pe.wait_ge(pt0_ready, n)
                        pe.wait_ge(pt1_ready, l * NBC + (b - 1) * UNITS + u)
                for c in range(1 if b == 0 else 2):
                    for kb_ in range(i + 1):
                        mm = pe.transpose(ps[:, pt_bank(b, u, c), kb_ * P:(kb_ + 1) * P],
                                          prob[u % 2][:, c, kb_ * P:(kb_ + 1) * P], ident[:])
                mm.then_inc(t_ready, 1)

            def values(l, b, u, p, i, w):
                n = l * NU + b * UNITS + u
                pe.wait_ge(pt0_ready, n + 1)
                if b:
                    pe.wait_ge(pt1_ready, l * NBC + (b - 1) * UNITS + u + 1)
                if u >= 2:
                    pe.wait_ge(ytok_ready, n - 1)
                for c in range(1 if b == 0 else 2):
                    for j in range(i + 1):
                        vals = (v[:, j, p * P:(p + 1) * P], bvw[:, j, 0:HD], v[:, j, p * P + c * HD:p * P + (c + 1) * HD])[b]
                        dst = ps[:, 6 + u % 2, 0:P] if b == 0 else ps[:, 6 + u % 2, c * HD:(c + 1) * HD]
                        mm = pe.matmul(dst, pt[u % 2][:, c, j, :], vals, start=(j == 0), stop=(j == i))
                mm.then_inc(o_ready, 1)

            def attention(l, b):
                pe.wait_ge(rope_ready, l * NROPE + ROPE_AT[b])
                for bank in range(RING):
                    pe.wait_ge(acc_free[bank], l * (NTILE // RING) + T_ATTENTION[b] // RING)
                every = list(units())
                for n in range(ITERATIONS):
                    if n < UNITS:
                        logits(l, b, *every[n])
                    gate_steps(l, b, n)
                    if 0 <= n - 1 < UNITS:
                        transposes(l, b, *every[n - 1])
                    if 0 <= n - 2:
                        values(l, b, *every[n - 2])

            def to_features(l, b, pairs):
                for p in pairs:
                    if b == 0:
                        pe.wait_ge(ynorm_ready, l * NPAIR + p + 1)
                    else:
                        pe.wait_ge(ytok_ready, l * NU + b * UNITS + (p + 1) * NT)
                    if p >= 2:
                        pe.wait_ge(y_split, l * 3 * NPAIR + b * NPAIR + p - 1)
                    for i in range(NT):
                        mm = pe.transpose(ps[:, 4 + p % 2, i * P:(i + 1) * P], ytok[:, p * NT + i, :], ident[:])
                    mm.then_inc(yt_ready, 1)

            def branch_product(l, b):
                pe.wait_ge(y_split, l * 3 * NPAIR + (b + 1) * NPAIR)
                for half in range(2):
                    feature_tiles(l, G_BRANCH[b] + half, T_BRANCH[b] + 4 * half, n=4, nk=KW, width=512, rhs=y)

            def projections(l, b):
                g, t = G_QKV[b], T_QKV[b]
                feature_tiles(l, g, t)
                if b == 0:
                    indexer(l, 1)
                feature_tiles(l, g + 1, t + 2, before_tile=(lambda i: to_features(l, b - 1, (2 * i, 2 * i + 1))) if b else None)
                if b != 1:
                    if b == 0:
                        indexer(l, 2)
                    feature_tiles(l, g + 2, t + 4)
                    if b == 0:
                        indexer(l, 3)
                    feature_tiles(l, g + 3, t + 6)
                    token_tiles(l, g + 4, t + 8, 2, 2, 256)
                    token_tiles(l, g + 5, t + 10, 2, 2, 256)

            with pe.Fori(0, DEPTH) as l:
                statistic(l, 0)
                group_wait(l, G_MISC)
                two_tiles_as_ready(G_MISC % 2, (T_MISC, T_MISC + 1), h_ready, l * 2 * KD, h, acc_ready)
                feature_tiles(l, G_MISC + 1, T_MISC + 2, n=1)
                token_tiles(l, G_MISC + 2, T_MISC + 3, 1, NT, P)
                projections(l, 0)
                for b in range(3):
                    attention(l, b)
                    pe.wait_ge(gate_free, l * 3 * KD + (b + 1) * KD)
                    if b < 2:
                        projections(l, b + 1)
                    else:
                        to_features(l, b, range(NPAIR))
                    branch_product(l, b)
                for bank in range(RING):
                    pe.wait_ge(acc_free[bank], l * (NTILE // RING) + T_FIN // RING)
                for g in range(4):
                    group_wait(l, G_OUT + g)
                    s = (G_OUT + g) % 2
                    if g == 0:
                        two_tiles_as_ready(s, (0, 1), m_split, l * KD, m_, y_ready)
                        continue
                    for i in range(2):
                        last = product(ps[:, 2 * g + i, :], [(*cols(s, kk, 256, i * P, P), kk) for kk in range(KD)], m_)
                        last.then_inc(group_done[s] if i else y_ready, 1)
                statistic(l, 1)
                def swiglu_in(i, j, between=None):
                    s = (G_FIN + i) % 2
                    pe.wait_ge(w_ready[s], l * (NG // 2) + j + ((G_FIN + i) // 2 + 1))
                    for a in range(2):
                        pe.wait_ge(acc_free[2 * i + a], l * (NTILE // RING) + j + T_FIN // RING)
                    two_tiles_as_ready(s, (2 * i, 2 * i + 1), h_ready, l * 2 * KD + KD, h, acc_ready, between)

                def norm_between(c):
                    if c == 4:
                        token_sums(l, 2)
                    if c == 6:
                        spread_inverse(l, 2)

                swiglu_in(0, 0)
                swiglu_in(1, 0, norm_between)
                with pe.Fori(1, KF // 2) as j:
                    for i in range(2):
                        swiglu_in(i, j)
                def ffn_out(s, rhs, first, final):
                    order = [*range(RING, KD), *range(RING)] if first else range(KD)
                    for m in order:
                        if first and m < RING:
                            pe.wait_ge(acc_free[m], l * (NTILE // RING) + NTILE // RING)
                        for kk in range(2):
                            wh, wl = cols(s, kk, D, m * P, P)
                            ah, al = rhs(kk)
                            pe.matmul(ps[:, m, :], wh, ah, start=(first and kk == 0), stop=False, skip_group_check=True)
                            pe.matmul(ps[:, m, :], wh, al, start=False, stop=False, skip_group_check=True)
                            last = pe.matmul(ps[:, m, :], wl, ah, start=False, stop=(final and kk == 1), skip_group_check=True)
                        if m == order[-1]:
                            last.then_inc(group_done[s], 1)
                        elif final:
                            last.then_inc(y_ready, 1)

                def act_static(k0):
                    return lambda kk: (ahi[:, k0 + kk, :], alo[:, k0 + kk, :])

                group_wait(l, G_FOUT)
                pe.wait_ge(act_split, l * KF + 2)
                ffn_out(G_FOUT % 2, act_static(0), True, False)
                with pe.Fori(0, 4) as j:
                    for i in range(2):
                        g = G_FOUT + 1 + i
                        if i == 0:
                            pe.wait_ge(act_split, l * KF + KF)
                        pe.wait_ge(w_ready[g % 2], l * (NG // 2) + j + (g // 2 + 1))
                        ffn_out(g % 2, lambda kk: tuple(a[:, bass.ds(j * 4 + (2 + 2 * i + kk), 1), :].rearrange("p a n -> p (a n)")
                                                        for a in (ahi, alo)), False, False)
                for i in range(2):
                    g = G_FOUT + 9 + i
                    group_wait(l, g)
                    ffn_out(g % 2, act_static(KF - 4 + 2 * i), False, i == 1)
                statistic(l, 3)

        @block.scalar
        def _(act):
            act.wait_ge(consts_made, 11)
            act.wait_ge(lam_dots_ready, 1)
            act.activation(lam_s[:], lam_s[:], ACT.Exp).then_inc(prelude_exp, 1)
            for i, (signed_angle, cos, sin) in enumerate(((res[0], cos64, sin64), (res[1], cos32, sin32))):
                act.wait_ge(angle_ready, 2 * i + 1)
                act.activation(sin[:], signed_angle[:], ACT.Sin).then_inc(sin_done, 1)
                act.wait_ge(angle_ready, 2 * i + 2)
                act.activation(cos[:], cos[:], ACT.Sin, scale=-1.0, bias=half_pi[:]).then_inc(sin_done, 1)

            def square(l, n, c, src):
                if c >= 3:
                    act.wait_ge(sum_ready, l * 4 * NSUM + n * NSUM + c - 2)
                act.activation(tmp[c % 3][:], src, ACT.Square).then_inc(sq_ready, 1)

            def load_sqrt():
                act.activation(unused[:, 0:1], eps[:], ACT.Sqrt)

            def deviation(l, n):
                act.wait_ge(stat_ready, l * 4 + n + 1)
                act.activation(dev[:], ps[:, STAT_BANK[n % 2], 0:NT], ACT.Sqrt, scale=1.0 / D, bias=eps[:]).then_inc(std_ready, 1)

            def pre_norm(l):
                for c in range(KD):
                    act.wait_ge(x_ready, l * 2 * KD + (X0 + c + 1 - KD))
                    square(l, 0, c, x[:, c, :])
                    if c == 2:
                        round_weights(l, G_MISC)
                deviation(l, 0)
                round_weights(l, G_MISC + 1)
                for c in range(KD):
                    act.wait_ge(pre_ready, l * KD + c + 1)
                    act.activation(hhi[:, c, :], tmp[1 + c % 2][:], ACT.Copy).then_inc(hhi_ready, 1)

            def ffn_input(l):
                for c in range(KD):
                    act.wait_ge(x_ready, l * 2 * KD + (X0 + c + 1))
                    act.activation(hhi[:, c, :], x[:, c, :], ACT.Copy, scale=g_cur[:, 2 * KD + c:2 * KD + c + 1]).then_inc(hhi_ready, 1)
                    square(l, 2, c, x[:, c, :])
                    if c == 2:
                        round_weights(l, G_FIN + 1)
                round_weights(l, G_FIN + 2)
                deviation(l, 2)

            def result_norm(l, n):
                act.drain()
                load_sqrt()
                for m in range(KD):
                    if n == 1 and m % 2 == 0 and m:
                        round_weights(l, G_OUT + m // 2 + 1)
                    how, count = Y_DONE[n // 2][m]
                    if how == "group":
                        act.wait_ge(group_done[count % 2], l * (NG // 2) + count // 2 + 1)
                    else:
                        act.wait_ge(y_ready, l * NY + count)
                    square(l, n, m, ps[:, m, :])
                deviation(l, n)

            def tile_wait(l, t):
                how, count = TILE_DONE[t]
                if how == "group":
                    act.wait_ge(group_done[count % 2], l * (NG // 2) + count // 2 + 1)
                else:
                    act.wait_ge(acc_ready, l * NACC + count)

            def round_weights(l, g):
                s, n = g % 2, g // 2
                act.wait_ge(raw_full[s], (l * (NG // 2) + (n + 1)) * 16)
                if n:
                    act.wait_ge(group_done[s], l * (NG // 2) + n)
                act.activation(whi[s][:], raw[s][:], ACT.Copy).then_inc(whi_ready[s], 1)

            def exponentials(l, b, u, p, i, w):
                n = l * NU + b * UNITS + u
                for c in range(2):
                    act.wait_ge(max_ready, l * NM + (b * MAPS + 2 * u + c + 1))
                    if u >= 2:
                        act.wait_ge(t_ready, n - 1)
                    act.activation(prob[u % 2][:, c, 0:w], ps[:, (2 * u + c) % SRING, 0:w], ACT.Exp,
                                   bias=negmax[:, u, c:c + 1], accum_out=esum[:, u, c:c + 1]).then_inc(exp_ready, 1)

            def keep_gate(l, b, m):
                g = G_GATE[b] + m // 2
                if m % 2:
                    act.wait_ge(group_done[g % 2], l * (NG // 2) + g // 2 + 1)
                else:
                    act.wait_ge(gate_ready, l * 3 * KD // 2 + (b * KD // 2 + m // 2 + 1))
                act.activation(gate[:, m, :], ps[:, GATE_BANK, :], ACT.Copy).then_inc(gate_free, 1)

            def copy_transposed(l, b, u, p, i, w):
                n = l * NU + b * UNITS + u
                act.wait_ge(t_ready, n + 1)
                if u >= 2:
                    act.wait_ge(o_ready, n - 1)
                bank = 4 + (u % 2 if b == 0 else 0)
                act.activation(pt[u % 2][:, 0, 0:i + 1, :], ps[:, bank, 0:w].rearrange("p (k q) -> p k q", q=P),
                               ACT.Copy).then_inc(pt0_ready, 1)

            def values(l, b):
                g, t = G_QKV[b], T_QKV[b]
                round_weights(l, g + 4)
                round_weights(l, g + 5)
                for n in range(4):
                    tile_wait(l, t + 8 + n)
                    vg, hf = n // 2, n % 2
                    act.activation(v[:, 2 * hf:2 * hf + 2, vg * 256:(vg + 1) * 256],
                                   ps[:, (t + n) % RING, :].rearrange("p (t n) -> p t n", t=2), ACT.Copy)\
                       .then_inc(acc_free[(t + n) % RING], 1)
                    if hf:
                        round_weights(l, g + 6 + vg)

            def high_results(l, b, pairs):
                for p in pairs:
                    act.wait_ge(yt_ready, l * 3 * NPAIR + b * NPAIR + p + 1)
                    act.activation(yhi[:, p, :], ps[:, 4 + p % 2, :], ACT.Copy).then_inc(yhi_ready, 1)

            with act.Fori(0, DEPTH) as l:
                act.drain()
                load_sqrt()
                pre_norm(l)
                round_weights(l, 2)
                round_weights(l, 3)
                tile_wait(l, T_MISC + 3)
                act.activation(bvw[:].rearrange("p t n -> p (t n)"), ps[:, (T_MISC + 3) % RING, :], ACT.Copy)\
                   .then_inc(acc_free[(T_MISC + 3) % RING], 1)
                round_weights(l, 4)
                round_weights(l, G_QKV[0] + 2)
                round_weights(l, G_QKV[0] + 3)
                values(l, 0)
                for b in range(3):
                    g = G_GATE[b] + 6
                    every = list(units())
                    for n in range(UNITS + 3):
                        if n < UNITS:
                            exponentials(l, b, *every[n])
                        for m in range(KD):
                            if n < ITERATIONS and GATE_STEPS[n] <= m * KD + KD - 1 < GATE_STEPS[n + 1]:
                                keep_gate(l, b, m)
                        if 0 <= n - 1 < UNITS:
                            copy_transposed(l, b, *every[n - 1])
                        for m in range(1, KD, 2):
                            if n < ITERATIONS and GATE_STEPS[n] <= m * KD + KD - 1 < GATE_STEPS[n + 1]:
                                round_weights(l, G_GATE[b] + m // 2 + 2)
                        if b == 0 and n >= 3:
                            u = n - 3
                            if u:
                                act.wait_ge(ysq_ready, l * UNITS + u)
                            act.wait_ge(ytok_ready, l * NU + u + 1)
                            act.activation(unused[:], ytok[:, u, :], ACT.Square, accum_out=ysq[:, u:u + 1]).then_inc(ysq_ready, 1)
                    if b == 0:
                        act.wait_ge(ysq_ready, l * UNITS + UNITS)
                        act.activation(ystd[:], ysq[:], ACT.Sqrt, scale=1.0 / (2 * HD), bias=eps[:]).then_inc(ystd_ready, 1)
                    high_results(l, b, (0, 1))
                    if b < 2:
                        round_weights(l, g)
                    high_results(l, b, (2, 3))
                    act.wait_ge(gate_free, l * 3 * KD + (b + 1) * KD)
                    for m in range(KD):
                        act.activation(gate[:, m, :], gate[:, m, :], ACT.Sigmoid).then_inc(sig_ready, 1)
                    if b < 2:
                        round_weights(l, g + 1)
                    if b == 1:
                        values(l, 2)
                    round_weights(l, G_BRANCH[b] + 2)
                    round_weights(l, G_BRANCH[b] + 3)
                result_norm(l, 1)
                ffn_input(l)
                with act.Fori(0, KF // 2) as j:
                    for i in range(2):
                        act.wait_ge(gate_scaled, l * KF + j * 2 + (i + 1))
                        act.activation(tmp[i][:], tmp[i][:], ACT.Silu).then_inc(silu_ready, 1)
                        s, n = (G_FIN + i + 1) % 2, (G_FIN + i + 3) // 2
                        act.wait_ge(raw_full[s], (l * (NG // 2) + j + (n + 1)) * 16)
                        act.wait_ge(group_done[s], l * (NG // 2) + j + n)
                        act.activation(whi[s][:], raw[s][:], ACT.Copy).then_inc(whi_ready[s], 1)
                for g in range(G_FOUT + 3, NG):
                    round_weights(l, g)
                result_norm(l, 3)

        @block.vector
        def _(dve):
            parts = two_pi_parts()
            dve.wait_ge(lam_loaded, 16)
            lam4 = lam_v[:].rearrange("p (l v) d -> p l v d", v=4)
            lam_q, lam_k = lam4[:, :, 0:2, :], lam4[:, :, 2:4, :]
            lam_p = tmp[0][:, 0:DEPTH * 2 * HD].rearrange("p (l v d) -> p l v d", l=DEPTH, v=2)
            dve.tensor_tensor(lam_p, lam_q, lam_k, ALU.mult)
            dve.drain()
            dve.tensor_reduce(lam_s[:], lam_p, axis=X, op=ALU.add).then_inc(lam_dots_ready, 1)
            dve.wait_ge(angle_loaded, 16 * 2)
            angle, turns = res
            dve.tensor_copy(turns[:], y0[:].bitcast(i32))
            dve.drain()
            dve.tensor_scalar(angle[:], turns[:], const[:, C_INV:C_INV + 1], None, ALU.mult)
            dve.drain()
            magic = 1.5 * 2 ** 23
            dve.tensor_scalar(turns[:], angle[:], 1 / (2 * math.pi), magic, ALU.mult, ALU.add)
            dve.drain()
            dve.tensor_scalar(turns[:], turns[:], magic, None, ALU.subtract)
            dve.drain()
            for part in parts:
                dve.scalar_tensor_tensor(angle[:], turns[:], -part, angle[:], ALU.mult, ALU.add)
                dve.drain()
            dve.tensor_scalar(angle[:], angle[:], -3.1415925, 3.1415925, ALU.max, ALU.min)
            dve.drain()
            dve.stream_shuffle(turns[:], angle[:], [*range(16, 24), *range(8, 16), *range(8), *range(24, 32)])
            for a, cos, sgn in ((angle, cos64, C_SGN64), (turns, cos32, C_SGN32)):
                dve.drain()
                dve.tensor_scalar(a[:], a[:], const[:, sgn:sgn + 1], None, ALU.mult).then_inc(angle_ready, 1)
                dve.drain()
                dve.scalar_tensor_tensor(cos[:], a[:], -1.0, a[:], ALU.mult, ALU.max).then_inc(angle_ready, 1)
            dve.wait_ge(small_loaded, 16 * 2)
            dve.wait_ge(prelude_exp, 1)
            for layer in range(DEPTH):
                dve.tensor_tensor(neglam_all[:, layer:layer + 1], lam_s[:, layer, 1:2], lam_s[:, layer, 0:1], ALU.subtract)
                dve.drain()
                dve.tensor_scalar(neglam_all[:, layer:layer + 1], neglam_all[:, layer:layer + 1], lam_init(layer), None, ALU.subtract)
                dve.tensor_scalar(subg_all[:, layer, :], subg_all[:, layer, :], 1.0 - lam_init(layer), None, ALU.mult)
            dve.wait_ge(sin_done, 4)

            swap = {n: [*range(n // 8, n // 4), *range(n // 8), *range(n // 4, 32)] for n in (64, 32)}

            def tile_wait(l, t):
                dve.drain()
                how, count = TILE_DONE[t]
                if how == "group":
                    dve.wait_ge(group_done[count % 2], l * (NG // 2) + count // 2 + 1)
                else:
                    dve.wait_ge(acc_ready, l * NACC + count)

            def rotate(l, t, dst, cos, sin, mask, scale=1.0):
                src = ps[:, t % RING, :]
                tile_wait(l, t)
                dve.scalar_tensor_tensor(tmp[2][:], src, scale, cos[:], ALU.mult, ALU.mult)
                dve.stream_shuffle(tmp[1][:], src, mask).then_inc(acc_free[t % RING], 1)
                dve.drain()
                dve.scalar_tensor_tensor(tmp[1][:], tmp[1][:], scale, sin[:], ALU.mult, ALU.mult)
                dve.drain()
                dve.tensor_tensor(dst, tmp[1][:], tmp[2][:], ALU.add).then_inc(rope_ready, 1)

            def inverse_deviation(l, n):
                dve.drain()
                dve.wait_ge(std_ready, l * 4 + n + 1)
                dve.reciprocal(inv[:], dev[:]).then_inc(inv_ready, 1)

            def pre_norm(l):
                inverse_deviation(l, 0)
                dve.wait_ge(rs_ready, l * 4 + 1)
                rs = ps[:, STAT_BANK[0], :]
                for c in range(KD + 1):
                    if c < KD:
                        if c >= 2:
                            dve.wait_ge(hhi_ready, l * 2 * KD + c - 1)
                            dve.wait_ge(h_ready, l * 2 * KD + c - 1)
                        dve.scalar_tensor_tensor(tmp[1 + c % 2][:], x[:, c, :], g_cur[:, c:c + 1], rs,
                                                 ALU.mult, ALU.mult).then_inc(pre_ready, 1)
                    if c >= 1:
                        dve.wait_ge(hhi_ready, l * 2 * KD + c)
                        dve.wait_ge(pre_ready, l * KD + c)
                        dve.tensor_tensor(hlo[:, c - 1, :], tmp[1 + (c - 1) % 2][:], hhi[:, c - 1, :].bitcast(f32),
                                          ALU.subtract).then_inc(h_ready, 1)

            def ffn_low(l, c):
                dve.wait_ge(hhi_ready, l * 2 * KD + (KD + c + 1))
                dve.scalar_tensor_tensor(hlo[:, c, :], x[:, c, :], g_cur[:, 2 * KD + c:2 * KD + c + 1], hhi[:, c, :].bitcast(f32),
                                         ALU.mult, ALU.subtract).then_inc(h_ready, 1)

            def result_norm(l, n):
                dve.drain()
                dve.wait_ge(sq_ready, l * 4 * KD + n * KD + 1)
                dve.tensor_copy(y0[:], ps[:, 0, :]).then_inc(y0_copied, 1)
                for c in range(1, KD):
                    dve.drain()
                    add_squares(dve, l, n, c)
                inverse_deviation(l, n)
                dve.wait_ge(rs_ready, l * 4 + n + 1)
                dve.tensor_copy(rs_res[:], ps[:, STAT_BANK[1], :])
                dve.drain()
                for c in range(KD):
                    if c >= 2:
                        dve.wait_ge(x_ready, l * 2 * KD + (X0 + (n // 2) * KD + c - 1))
                    src = y0[:] if c == 0 else ps[:, c, :]
                    dve.scalar_tensor_tensor(res[c % 2][:], src, g_cur[:, n * KD + c:n * KD + c + 1], rs_res[:],
                                             ALU.mult, ALU.mult)
                    dve.drain()
                    dve.tensor_tensor(x[:, c, :], x[:, c, :], res[c % 2][:], ALU.add).then_inc(x_ready, 1)
                    if n == 1 and c:
                        ffn_low(l, c - 1)
                if n == 1:
                    ffn_low(l, KD - 1)

            def index_scores(l, i):
                w = (i + 1) * P
                score, term = scores[:, WMASK[i - 1]:WMASK[i]], tmp[0][:, 0:w]
                dve.drain()
                dve.wait_ge(idx_ready, l * (NT - 1) + i)
                if i == 1:
                    dve.wait_ge(acc_free[(T_MISC + 3) % RING], l * (NTILE // RING) + 1)
                for hh in range(4):
                    op = dve.tensor_scalar(term if hh else score, ps[:, 4 + hh, 0:w], 0.0, bvw[:, i, HD + hh:HD + hh + 1],
                                           ALU.max, ALU.mult)
                    if hh == 3:
                        op.then_inc(idx_used, 1)
                    dve.drain()
                    if hh:
                        dve.tensor_tensor(score, score, term, ALU.add)
                        dve.drain()
                past = scores[:, WMASK[i] - P:WMASK[i]]
                dve.tensor_tensor(past, past, causal[:], ALU.add)

            def top_k_rounds(first, n):
                for r in range(first, first + n):
                    i = 1 + r // ROUNDS
                    score = scores[:, WMASK[i - 1]:WMASK[i]]
                    dve.drain()
                    dve.max(out=top8[:], in_=score)
                    dve.drain()
                    dve.match_replace(out=score, in_to_replace=top8[:], in_values=score, imm_value=TAKEN)
                    if r % ROUNDS == ROUNDS - 1:
                        dve.drain()
                        dve.tensor_scalar(maskb[:, WMASK[i - 1]:WMASK[i]], score, TAKEN / 2, -BIG, ALU.is_gt, ALU.mult)\
                           .then_inc(mask_ready, 1)

            def maxima(l, b, u, p, i, w):
                for c in range(2):
                    dve.drain()
                    m = 2 * u + c
                    dve.wait_ge(s_ready, l * NM + (b * MAPS + m + 1))
                    dve.tensor_reduce(negmax[:, u, c:c + 1], ps[:, m % SRING, 0:w], axis=X, op=ALU.max, negate=True)\
                       .then_inc(max_ready, 1)

            def after_exp(l, b, u, p, i, w):
                dve.drain()
                dve.wait_ge(exp_ready, l * NM + (b * MAPS + 2 * u + 2))
                dve.reciprocal(rinv[:, u, :], esum[:, u, :])
                if b == 0:
                    pr = prob[u % 2]
                    dve.drain()
                    dve.scalar_tensor_tensor(ratio[:], esum[:, u, 0:1], rinv[:, u, 1:2], neglam[:], ALU.mult, ALU.mult)
                    dve.drain()
                    dve.scalar_tensor_tensor(pr[:, 0, 0:w], pr[:, 1, 0:w], ratio[:], pr[:, 0, 0:w],
                                             ALU.mult, ALU.add).then_inc(diff_ready, 1)

            def copy_transposed(l, b, u, p, i, w):
                n = l * NU + b * UNITS + u
                dve.wait_ge(t_ready, n + 1)
                if u >= 2:
                    dve.wait_ge(o_ready, n - 1)
                dve.tensor_copy(pt[u % 2][:, 1, 0:i + 1, :], ps[:, 5, 0:w].rearrange("p (k q) -> p k q", q=P)).then_inc(pt1_ready, 1)

            def results(l, b, u, p, i, w):
                dve.wait_ge(o_ready, l * NU + b * UNITS + u + 1)
                o = ps[:, 6 + u % 2, :]
                if b == 0:
                    op = dve.tensor_scalar(ytok[:, u, :], o[:, 0:P], rinv[:, u, 0:1], None, ALU.mult)
                else:
                    for c in range(2):
                        op = dve.tensor_scalar(ytok[:, u, c * HD:(c + 1) * HD], o[:, c * HD:(c + 1) * HD],
                                               rinv[:, u, c:c + 1], None, ALU.mult)
                op.then_inc(ytok_ready, 1)

            def low_results(l, b, pairs):
                for p in pairs:
                    dve.wait_ge(yhi_ready, l * 3 * NPAIR + b * NPAIR + p + 1)
                    dve.tensor_tensor(ylo[:, p, :], ps[:, 4 + p % 2, :], yhi[:, p, :].bitcast(f32), ALU.subtract).then_inc(y_split, 1)

            def projections(l, b):
                for i in range(4):
                    rotate(l, T_QKV[b] + i, q[:, i, :], cos64, sin64, swap[64], SCALE)
                    if b and i in (1, 2):
                        low_results(l, b - 1, (2 * i - 2, 2 * i - 1))
                    if b == 0 and i in (1, 3):
                        index_scores(l, (i + 1) // 2)
                if b != 1:
                    for i in range(4):
                        rotate(l, T_QKV[b] + 4 + i, k[:, i, :], cos64, sin64, swap[64])
                        if b == 0 and i == 1:
                            index_scores(l, 3)

            with dve.Fori(0, DEPTH) as l:
                dve.drain()
                dve.tensor_copy(g_cur[:], g_all[:, bass.ds(l, 1), :].rearrange("p a n -> p (a n)"))
                dve.tensor_copy(subg[:], subg_all[:, bass.ds(l, 1), :].rearrange("p a n -> p (a n)"))
                dve.tensor_copy(neglam[:], neglam_all[:, bass.ds(l, 1)])
                dve.drain()
                pre_norm(l)
                rotate(l, T_MISC, kb[:], cos64, sin64, swap[64])
                rotate(l, T_MISC + 1, ik[:], cos32, sin32, swap[32])
                rotate(l, T_MISC + 2, iq[:], cos32, sin32, swap[32])
                projections(l, 0)
                top_k_rounds(0, 20)
                for b in range(3):
                    every = list(units())
                    for n in range(ITERATIONS):
                        if 1 <= n <= UNITS:
                            after_exp(l, b, *every[n - 1])
                        if n < UNITS:
                            maxima(l, b, *every[n])
                        if b == 0 and n < 14:
                            top_k_rounds(20 + 2 * n, 2)
                        if b and 0 <= n - 1 < UNITS:
                            copy_transposed(l, b, *every[n - 1])
                        if n >= 2:
                            results(l, b, *every[n - 2])
                    if b == 0:
                        dve.wait_ge(ystd_ready, l + 1)
                        dve.reciprocal(yrs[:], ystd[:])
                        dve.drain()
                        for u, p, i, w in units():
                            op = dve.scalar_tensor_tensor(ytok[:, u, :], ytok[:, u, :], yrs[:, u:u + 1], subg[:], ALU.mult, ALU.mult)
                            if i == NT - 1:
                                op.then_inc(ynorm_ready, 1)
                    if b < 2:
                        projections(l, b + 1)
                    else:
                        low_results(l, b, range(NPAIR))
                    for m in range(KD):
                        t = T_BRANCH[b] + m
                        tile_wait(l, t)
                        dve.wait_ge(sig_ready, l * 3 * KD + (b * KD + m + 1))
                        dst = merged[:, m, :] if b == 0 else tmp[1][:]
                        dve.tensor_tensor(dst, ps[:, t % RING, :], gate[:, m, :], ALU.mult)\
                           .then_inc(acc_free[t % RING], 1)
                        if b:
                            dve.drain()
                            dve.tensor_tensor(merged[:, m, :], merged[:, m, :], tmp[1][:], ALU.add)
                        if b == 2:
                            dve.drain()
                            dve.tensor_copy(mhi[:, m, :], merged[:, m, :])
                            dve.drain()
                            dve.tensor_tensor(mlo[:, m, :], merged[:, m, :], mhi[:, m, :].bitcast(f32), ALU.subtract).then_inc(m_split, 1)
                result_norm(l, 1)
                inverse_deviation(l, 2)
                dve.wait_ge(rs_ready, l * 4 + 3)
                dve.tensor_copy(rs_ffn[:], ps[:, STAT_BANK[0], :])
                with dve.Fori(0, KF // 2) as j:
                    for i in range(2):
                        dve.drain()
                        dve.wait_ge(acc_ready, l * NACC + j * 2 + (ACC_FIN + i))
                        dve.tensor_tensor(tmp[i][:], ps[:, 2 * i, :], rs_ffn[:], ALU.mult).then_inc(gate_scaled, 1)
                        dve.wait_ge(group_done[(G_FIN + i) % 2], l * (NG // 2) + j + ((G_FIN + i) // 2 + 1))
                        dve.wait_ge(gate_scaled, l * KF + j * 2 + (i + 1))
                        dve.tensor_tensor(tmp[2][:], ps[:, 2 * i + 1, :], rs_ffn[:], ALU.mult).then_inc(acc_free[2 * i + 1], 1)
                        dve.drain()
                        dve.wait_ge(silu_ready, l * KF + j * 2 + (i + 1))
                        f = bass.ds(j * 2 + i, 1)
                        ah, al = (a[:, f, :].rearrange("p a n -> p (a n)") for a in (ahi, alo))
                        dve.tensor_tensor(tmp[2][:], tmp[i][:], tmp[2][:], ALU.mult).then_inc(acc_free[2 * i], 1)
                        dve.drain()
                        dve.tensor_copy(ah, tmp[2][:])
                        dve.drain()
                        dve.tensor_tensor(al, tmp[2][:], ah.bitcast(f32), ALU.subtract).then_inc(act_split, 1)
                result_norm(l, 3)


def groups(a, width):
    kk = GCOLS // width
    kdim, n = a.shape
    a = a.reshape(kdim // (P * kk), kk, P, n // width, width)
    return a.transpose(3, 0, 2, 1, 4).reshape(-1, P, GCOLS)


def weight_stream(w_in, w_branch, w_out, w_ffn_in, w_ffn_out):
    stream = []
    for layer in range(DEPTH):
        w = w_in[layer]
        cut = np.cumsum([0, 512, 512, 512, 512, HD, HD, 128, 32, 4, 512, 512, 512])
        aq, ak, av, bq, bk, bv, iq, ik, iw, cq, ck, cv = (w[:, cut[i]:cut[i] + n] for i, n in enumerate(
            (512, 512, 512, 512, HD, HD, 128, 32, 4, 512, 512, 512)))
        misc = [bk, bk, ik, ik, ik, ik, iq, iq] + ([bv] + [iw] * 16) * 2
        stream.append(groups(np.concatenate(misc, axis=1), 256))
        qkv = ([aq, ak, av], [bq], [cq, ck, cv])
        stream.append(groups(np.concatenate(qkv[0], axis=1), 256))
        for b in range(3):
            stream.append(groups(w[:, cut[-1] + b * D:cut[-1] + (b + 1) * D], 256))
            if b < 2:
                stream.append(groups(np.concatenate(qkv[b + 1], axis=1), 256))
            stream.append(groups(w_branch[layer, b], 512))
        stream.append(groups(w_out[layer], 256))
        fin = w_ffn_in[layer].reshape(D, 2, KF, P).transpose(0, 2, 1, 3).reshape(D, 2 * FF)
        stream += [groups(fin, 256), groups(w_ffn_out[layer], D)]
    return np.ascontiguousarray(np.concatenate(stream))


def constants():
    c = np.zeros((P, NCONST), np.float32)
    for n, sgn, first in ((64, C_SGN64, 0), (32, C_SGN32, 16)):
        rot = n // 4
        freq = np.power(np.float32(500000.0), -np.arange(rot // 2, dtype=np.float32) * np.float32(2.0) / np.float32(rot))
        for p in range(P):
            if first <= p % 32 < first + rot:
                c[p, C_INV] = freq[(p % 32 - first) % (rot // 2)]
            if p % n < rot:
                c[p, sgn] = -1.0 if p % n < rot // 2 else 1.0
    return c


def kernel(x, positions, w_in, w_branch, w_out, lambda_q1, lambda_k1, lambda_q2, lambda_k2, subln_g, norm_g,
           w_ffn_in, w_ffn_out):
    import concourse.bacc as bacc
    from concourse.bass_utils import run_bass_kernel_spmd

    x, w_in, w_branch, w_out, w_ffn_in, w_ffn_out = map(np.asarray, (x, w_in, w_branch, w_out, w_ffn_in, w_ffn_out))
    lam = np.stack([np.asarray(a) for a in (lambda_q1, lambda_q2, lambda_k1, lambda_k2)], axis=1)
    arrays = {
        "x_in": np.ascontiguousarray(x[0].T.reshape(KD, P, SEQ).transpose(1, 0, 2)),
        "pos_in": np.ascontiguousarray(np.asarray(positions)),
        "w_in": weight_stream(w_in, w_branch, w_out, w_ffn_in, w_ffn_out),
        "lam_in": np.ascontiguousarray(lam.reshape(1, -1)),
        "subg_in": np.ascontiguousarray(np.asarray(subln_g).reshape(1, -1)),
        "g_in": np.ascontiguousarray(np.asarray(norm_g).reshape(DEPTH, 4 * KD, P).transpose(2, 0, 1)),
        "const_in": constants(),
    }
    nc = bacc.Bacc("TRN2", target_bir_lowering=False, num_devices=1,
                   dynamic_dma_scratch_size=1024)
    args = [nc.dram_tensor(n, a.shape, mybir.dt.from_np(a.dtype), kind="ExternalInput").ap() for n, a in arrays.items()]
    out = nc.dram_tensor("out", (P, KD, SEQ), mybir.dt.float32, kind="ExternalOutput").ap()
    trunk(nc, *args, out)
    r = run_bass_kernel_spmd(nc, [arrays], core_ids=[0])
    got = np.asarray(r.results[0]["out"])
    return np.ascontiguousarray(got.transpose(1, 0, 2).reshape(D, SEQ).T)[None]
```

```python
import math
from contextlib import ExitStack

import numpy as np

import concourse.bass as bass
from concourse import mybir
from concourse.alu_op_type import AluOpType as ALU

P = 128
DEPTH, SEQ, D = 2, 512, 1024
KD = D // P
NT = SEQ // P
HD = 64
NPAIR = 4
WIDTH = 512
KW = WIDTH // P
FF = 2816
KF = FF // P
TOPK = min(256, SEQ // 4)
EPS = 1e-6
SCALE = HD ** -0.5
GCOLS = 2048
ARENA_KIB = 96
BIG = 1e30
TAKEN = -3e38

G_MISC = 0
G_QKV = (3, 13, 21)
G_GATE = (9, 17, 29)
G_BRANCH = (15, 27, 33)
G_OUT = 35
G_FIN = 39
G_FOUT = 61
NG = 72

T_MISC = 0
T_QKV = (4, 16, 28)
T_BRANCH = (20, 40, 48)
T_ATTENTION = (16, 28, 48)
T_FIN = 56
NTILE = 100
RING = 4
GATE_BANK = 3
NSUM = KD - 1
STAT_BANK = (4, 0)
SRING = 3

TILES_OF = dict([(0, 2), (1, 1), (2, 1)]
                + [(g, 2) for b, n in enumerate((6, 2, 6)) for g in range(G_QKV[b], G_QKV[b] + n)]
                + [(g, 4) for b in range(3) for g in (G_BRANCH[b], G_BRANCH[b] + 1)]
                + [(g, 2) for g in range(G_FIN, G_FOUT)])
TILE_DONE, NACC = [], 0
for _g in sorted(TILES_OF):
    for _i in range(TILES_OF[_g]):
        if _i == TILES_OF[_g] - 1:
            TILE_DONE.append(("group", _g))
        else:
            NACC += 1
            TILE_DONE.append(("tile", NACC))
ACC_FIN = TILE_DONE[T_FIN][1]
assert len(TILE_DONE) == NTILE
Y_DONE = ([("tile", m // 2 + 1) if m % 2 == 0 else ("group", G_OUT + m // 2) for m in range(KD)],
          [("tile", KD // 2 + m + 1) if m < KD - 1 else ("group", NG - 1) for m in range(KD)])
NY = KD // 2 + KD - 1

X0 = KD
ROPE_AT = (11, 15, 23)
NROPE = 23
NIDX = 3
UNITS = NPAIR * NT
NU = 3 * UNITS
MAPS = 2 * UNITS
NM = 3 * MAPS
ROUNDS = TOPK // 8
WMASK = [0, 2 * P, 5 * P, 9 * P]
NBC = 2 * UNITS
TOPK_AT = (1, 2, 4, 5, 6, 9, 10, 13, 14)
ITERATIONS = UNITS + 2
GATE_SPANS = (2, 2, 2, 2, 2, 3, 2, 3)
GATE_STEPS = [m * KD + KD * n // span for m, span in enumerate(GATE_SPANS) for n in range(span)] + [KD * KD]
assert len(GATE_STEPS) == ITERATIONS + 1

C_INV, C_SGN64, C_SGN32, NCONST = 0, 1, 2, 3


def lam_init(layer):
    return 0.8 - 0.6 * math.exp(-0.3 * layer)


def two_pi_parts():
    left, parts = 2 * math.pi, []
    for _ in range(3):
        step = 2.0 ** (math.floor(math.log2(left)) - 7)
        parts.append(math.floor(left / step) * step)
        left -= parts[-1]
    return parts + [left]


def trunk(nc, x_in, pos_in, w_in, lam_in, subg_in, g_in, const_in, out):
    f32, f32r, bf16, i32 = mybir.dt.float32, mybir.dt.float32r, mybir.dt.bfloat16, mybir.dt.int32
    ACT = mybir.ActivationFunctionType
    X = mybir.AxisListType.X
    ctx = ExitStack()
    with ctx:
        def sb(name, shape, dt=f32):
            return ctx.enter_context(nc.sbuf_tensor(name, shape, dt))

        def sem(name):
            return ctx.enter_context(nc.semaphore(name))

        x = sb("x", [P, KD, SEQ])
        hhi = sb("hhi", [P, KD, SEQ], f32r)
        hlo = sb("hlo", [P, KD, SEQ], f32r)
        raw = [sb(f"raw{s}", [P, GCOLS]) for s in range(2)]
        whi = [sb(f"whi{s}", [P, GCOLS], f32r) for s in range(2)]
        wlo = [sb(f"wlo{s}", [P, GCOLS], f32r) for s in range(2)]
        cos64, sin64, cos32, sin32 = (sb(n, [P, SEQ]) for n in ("cos64", "sin64", "cos32", "sin32"))
        tmp = [sb(f"tmp{i}", [P, SEQ]) for i in range(3)]
        ident = sb("ident", [P, P])
        identb = sb("identb", [P, P], bf16)
        causal = sb("causal", [P, P])
        causalb = sb("causalb", [P, P], bf16)
        ones = sb("ones", [P, P])
        const = sb("const", [P, NCONST])
        eps = sb("eps", [P, 1])
        half_pi = sb("half_pi", [P, 1])
        cos64r, sin64r = sb("cos64r", [P, SEQ]), sb("sin64r", [P, SEQ])
        g_all = sb("g_all", [P, DEPTH, 5 * KD])
        g_cur = sb("g_cur", [P, 5 * KD])
        g0 = sb("g0", [P, KD])
        subg_all = sb("subg_all", [P, DEPTH, P])
        subg = sb("subg", [P, P])
        lam_s = sb("lam_s", [P, DEPTH, 2])
        neglam_all = sb("neglam_all", [P, DEPTH])
        neglam = sb("neglam", [P, 1])
        negmax = sb("negmax", [P, UNITS, 2])
        esum = sb("esum", [P, UNITS, 2])
        rinv = sb("rinv", [P, UNITS, 2])
        ratio = sb("ratio", [P, 1])
        started = sb("started", [P, 1])
        dev = sb("dev", [P, NT])
        inv = sb("inv", [P, NT])
        ysq = sb("ysq", [P, UNITS])
        ystd = sb("ystd", [P, UNITS])
        yrs = sb("yrs", [P, UNITS])
        top8 = sb("top8", [P, 8 * (NT - 1)])
        kb = sb("kb", [P, SEQ])
        sumsq = kb
        y0 = sb("y0", [P, SEQ])
        unused = sb("unused", [P, P])

        arena_at = -(-nc.sbuf_base // 32) * 32
        sb("arena", [P, ARENA_KIB * 256])
        assert nc.sbuf_base == arena_at + ARENA_KIB * 1024

        def at(name, kib, shape, dt=f32):
            return nc.alloc_sbuf_tensor_at(name, shape, dt, offset=arena_at + kib * 1024)

        lam_v = at("lam_v", 0, [P, DEPTH * 4, HD])
        q = at("q", 0, [P, NPAIR, SEQ])
        k = at("k", 8, [P, NPAIR, SEQ])
        v = at("v", 16, [P, NT, WIDTH])
        iq = at("iq", 24, [P, SEQ])
        ik = at("ik", 26, [P, SEQ])
        bvf = y0
        bvw = at("bvw", 28, [P, NT, P])
        maskb = at("maskb", 30, [P, WMASK[-1]], bf16)
        scores = at("scores", 33, [P, WMASK[-1]])
        ytok = at("ytok", 38, [P, UNITS, P])
        prob = [at(f"prob{i}", 46 + 4 * i, [P, 2, SEQ]) for i in range(2)]
        cos32r, sin32r = at("cos32r", 46, [P, SEQ]), at("sin32r", 48, [P, SEQ])
        pt = [at(f"pt{i}", 54 + 4 * i, [P, 2, NT, P]) for i in range(2)]
        yhi = at("yhi", 46, [P, KW, SEQ], f32r)
        ylo = at("ylo", 54, [P, KW, SEQ], f32r)
        gate = at("gate", 62, [P, KD, SEQ])
        merged = at("merged", 78, [P, KD, SEQ])
        mhi = at("mhi", 0, [P, KD, SEQ], f32r)
        mlo = at("mlo", 16, [P, KD, SEQ], f32r)
        rs_res = at("rs_res", 88, [P, SEQ])
        res = [at(f"res{i}", 90 + 2 * i, [P, SEQ]) for i in range(2)]
        rs_h = at("rs_h", 94, [P, SEQ])
        ahi = at("ahi", 0, [P, KF, SEQ], f32r)
        alo = at("alo", 44, [P, KF, SEQ], f32r)

        ps = ctx.enter_context(nc.psum_tensor("ps", [P, 8, SEQ], f32))

        x_loaded = sem("x_loaded")
        lam_loaded, angle_loaded, small_loaded, stored = sem("lam_loaded"), sem("angle_loaded"), sem("small_loaded"), sem("stored")
        consts_made, lam_dots_ready, prelude_exp = sem("consts_made"), sem("lam_dots_ready"), sem("prelude_exp")
        angle_ready, sin_done = sem("angle_ready"), sem("sin_done")
        raw_full = [sem(f"raw_full{s}") for s in range(2)]
        whi_ready = [sem(f"whi_ready{s}") for s in range(2)]
        w_ready = [sem(f"w_ready{s}") for s in range(2)]
        group_done = [sem(f"group_done{s}") for s in range(2)]
        acc_ready = sem("acc_ready")
        acc_free = [sem(f"acc_free{b}") for b in range(RING)]
        sq_ready, sum_ready, stat_ready, std_ready = sem("sq_ready"), sem("sum_ready"), sem("stat_ready"), sem("std_ready")
        inv_ready, rs_ready = sem("inv_ready"), sem("rs_ready")
        g0_ready, hhi_ready, h_ready, x_ready = sem("g0_ready"), sem("hhi_ready"), sem("h_ready"), sem("x_ready")
        res_ready = sem("res_ready")
        y_ready, y0_copied = sem("y_ready"), sem("y0_copied")
        rope_ready = sem("rope_ready")
        bvt_ready, bvw_ready = sem("bvt_ready"), sem("bvw_ready")
        idx_ready, idx_used, mask_ready = sem("idx_ready"), sem("idx_used"), sem("mask_ready")
        s_ready, max_ready, exp_ready, diff_ready = sem("s_ready"), sem("max_ready"), sem("exp_ready"), sem("diff_ready")
        t_ready, pt0_ready, pt1_ready = sem("t_ready"), sem("pt0_ready"), sem("pt1_ready")
        o_ready, ytok_ready, ysq_ready, ystd_ready = sem("o_ready"), sem("ytok_ready"), sem("ysq_ready"), sem("ystd_ready")
        ynorm_ready, yt_ready, yhi_ready, y_split = sem("ynorm_ready"), sem("yt_ready"), sem("yhi_ready"), sem("y_split")
        m_split = sem("m_split")
        gate_rs_ready = sem("gate_rs_ready")
        gate_scaled, silu_ready = sem("gate_scaled"), sem("silu_ready")
        act_split = sem("act_split")
        gate_ready, gate_free, sig_ready = sem("gate_ready"), sem("gate_free"), sem("sig_ready")

        def add_squares(eng, l, n, c):
            eng.wait_ge(sq_ready, l * 4 * KD + n * KD + c + 1)
            eng.tensor_tensor(sumsq[:], sumsq[:] if c > 1 else tmp[0][:], tmp[c % 3][:], ALU.add).then_inc(sum_ready, 1)

        def gate_wait(eng, l, b, m):
            g = G_GATE[b] + m // 2
            if m % 2:
                eng.wait_ge(group_done[g % 2], l * (NG // 2) + g // 2 + 1)
            else:
                eng.wait_ge(gate_ready, l * 3 * KD // 2 + (b * KD // 2 + m // 2 + 1))

        def completes(n, m):
            return GATE_STEPS[n] < (m + 1) * KD <= GATE_STEPS[n + 1]

        def units():
            for u in range(UNITS):
                yield u, u // NT, u % NT, (u % NT + 1) * P

        block = ctx.enter_context(nc.Block())

        @block.sync
        def _(sp):
            sp.dma_start(lam_v[:].rearrange("p l n -> p (l n)"), lam_in.to_broadcast([P, DEPTH * 4 * HD])).then_inc(lam_loaded, 16)
            sp.dma_start(const[:], const_in).then_inc(angle_loaded, 16)
            sp.dma_start(y0[:].bitcast(i32), pos_in.to_broadcast([P, SEQ])).then_inc(angle_loaded, 16)
            sp.dma_start(x[:], x_in).then_inc(x_loaded, 16)
            sp.dma_start(raw[0][:], w_in[0]).then_inc(raw_full[0], 16)
            sp.dma_start(g_all[:], g_in).then_inc(small_loaded, 16)
            sp.dma_start(subg_all[:].rearrange("p l n -> p (l n)"), subg_in.to_broadcast([P, DEPTH * P])).then_inc(small_loaded, 16)
            sp.dma_start(raw[1][:], w_in[1]).then_inc(raw_full[1], 16)
            with sp.Fori(1, DEPTH * NG // 2) as j:
                for s in range(2):
                    sp.wait_ge(w_ready[s], j)
                    sp.dma_start(raw[s][:], w_in[bass.ds(j * 2 + s, 1), :, :].rearrange("g p n -> (g p) n")).then_inc(raw_full[s], 16)
            for c in range(KD):
                sp.wait_ge(x_ready, X0 + DEPTH * 2 * KD - KD + c + 1)
                sp.dma_start(out[:, c, :], x[:, c, :]).then_inc(stored, 16)
            sp.wait_ge(stored, 16 * KD)

        @block.gpsimd
        def _(pool):
            for t in (ident, identb, causal, causalb):
                pool.memset(t[:], 0.0).then_inc(consts_made, 1)
            pool.memset(ones[:], 1.0).then_inc(consts_made, 1)
            pool.memset(eps[:], EPS).then_inc(consts_made, 1)
            pool.memset(half_pi[:], math.pi / 2).then_inc(consts_made, 1)
            pool.wait_ge(consts_made, 7)
            for t in (ident, identb):
                pool.affine_select(out=t[:], in_=t[:], compare_op=ALU.not_equal, fill=1.0, base=0,
                                   pattern=[[-1, P]], channel_multiplier=1).then_inc(consts_made, 1)
            for t in (causal, causalb):
                pool.affine_select(out=t[:], in_=t[:], compare_op=ALU.is_ge, fill=-BIG, base=0,
                                   pattern=[[-1, P]], channel_multiplier=1).then_inc(consts_made, 1)
            pool.wait_ge(x_loaded, 16)
            pool.memset(started[:], 0.0).then_inc(x_ready, X0)

            def low_weights(l, n, s):
                pool.wait_ge(whi_ready[s], l * (NG // 2) + n + 1)
                pool.tensor_tensor(wlo[s][:], raw[s][:], whi[s][:].bitcast(f32), ALU.subtract).then_inc(w_ready[s], 1)

            def sum_squares(l, n, chunks=range(1, KD)):
                for c in chunks:
                    pool.drain()
                    add_squares(pool, l, n, c)

            with pool.Fori(0, DEPTH) as l:
                low_weights(l, 0, 0)
                sum_squares(l, 0)
                low_weights(l, 0, 1)
                with pool.Fori(1, G_FIN // 2 + 1) as n:
                    for s in range(2):
                        low_weights(l, n, s)
                sum_squares(l, 2, range(1, 5))
                low_weights(l, (G_FIN + 1) // 2, 0)
                sum_squares(l, 2, range(5, KD))
                low_weights(l, (G_FIN + 1) // 2, 1)
                with pool.Fori((G_FIN + 1) // 2 + 1, NG // 2) as n:
                    for s in range(2):
                        low_weights(l, n, s)

        @block.tensor
        def _(pe):
            pe.wait_ge(consts_made, 11)

            def group_wait(l, g):
                pe.wait_ge(w_ready[g % 2], l * (NG // 2) + g // 2 + 1)

            def bank_wait(l, t):
                if t >= RING:
                    pe.wait_ge(acc_free[t % RING], l * (NTILE // RING) + t // RING)

            def product(dst, terms, rhs, first=True, final=True):
                rhi, rlo = rhs
                n = len(terms)
                for i, (wh, wl, c) in enumerate(terms):
                    pe.matmul(dst, wh, rhi(c), start=(first and i == 0), stop=False)
                    pe.matmul(dst, wh, rlo(c), start=False, stop=False)
                    last = pe.matmul(dst, wl, rhi(c), start=False, stop=(final and i == n - 1))
                return last

            def cols(s, kk, width, c0, n):
                o = kk * width + c0
                return whi[s][:, o:o + n], wlo[s][:, o:o + n]

            h = (lambda c: hhi[:, c, :], lambda c: hlo[:, c, :])
            y = (lambda c: yhi[:, c, :], lambda c: ylo[:, c, :])
            m_ = (lambda c: mhi[:, c, :], lambda c: mlo[:, c, :])

            def two_tiles_as_ready(s, banks, chunk_ready, before, rhs, first_done, between=None):
                rhi, rlo = rhs
                for c in range(KD):
                    if between:
                        between(c)
                    pe.wait_ge(chunk_ready, before + (c + 1))
                    for a, bank in enumerate(banks):
                        wh, wl = cols(s, c, 256, a * P, P)
                        pe.matmul(ps[:, bank, :], wh, rhi(c), start=(c == 0), stop=False, skip_group_check=True)
                        pe.matmul(ps[:, bank, :], wh, rlo(c), start=False, stop=False, skip_group_check=True)
                        last = pe.matmul(ps[:, bank, :], wl, rhi(c), start=False, stop=(c == KD - 1), skip_group_check=True)
                        if c == KD - 1:
                            last.then_inc(group_done[s] if a else first_done, 1)

            def feature_tiles(l, g, t, n=2, nk=KD, width=256, rhs=h, before_tile=None):
                group_wait(l, g)
                for i in range(n):
                    if before_tile:
                        before_tile(i)
                    bank_wait(l, t + i)
                    last = product(ps[:, (t + i) % RING, :],
                                   [(*cols(g % 2, kk, width, i * P, P), kk) for kk in range(nk)], rhs)
                    last.then_inc(group_done[g % 2] if i == n - 1 else acc_ready, 1)

            def token_tiles(l, g, t, ntile, per, width):
                group_wait(l, g)
                s = g % 2
                for i in range(ntile):
                    bank_wait(l, t + i)
                    for j in range(per):
                        tt = i * per + j
                        dst = ps[:, (t + i) % RING, j * width:(j + 1) * width]
                        for kk in range(KD):
                            hh, hl = (a[:, kk, tt * P:(tt + 1) * P] for a in (hhi, hlo))
                            wh, wl = (a[s][:, kk * 256:kk * 256 + width] for a in (whi, wlo))
                            pe.matmul(dst, hh, wh, start=(kk == 0), stop=False)
                            pe.matmul(dst, hh, wl, start=False, stop=False)
                            last = pe.matmul(dst, hl, wh, start=False, stop=(kk == KD - 1))
                    last.then_inc(group_done[s] if i == ntile - 1 else acc_ready, 1)

            def token_sums(l, n):
                if n % 2:
                    pe.wait_ge(y0_copied, l * 2 + n // 2 + 1)
                pe.wait_ge(sum_ready, l * 4 * NSUM + (n + 1) * NSUM)
                for j in range(NT):
                    mm = pe.matmul(ps[:, STAT_BANK[n % 2], j:j + 1], sumsq[:, j * P:(j + 1) * P], ones[:, 0:1], start=True, stop=True)
                mm.then_inc(stat_ready, 1)

            def spread_inverse(l, n):
                pe.wait_ge(inv_ready, l * 4 + n + 1)
                for j in range(NT):
                    mm = pe.matmul(ps[:, STAT_BANK[n % 2], j * P:(j + 1) * P], inv[:, j:j + 1].to_broadcast([P, P]), ident[:],
                                   start=True, stop=True)
                mm.then_inc(rs_ready, 1)

            def statistic(l, n):
                token_sums(l, n)
                spread_inverse(l, n)

            def indexer(l, i):
                pe.wait_ge(rope_ready, l * NROPE + NIDX)
                if i > 1:
                    pe.wait_ge(idx_used, l * (NT - 1) + i - 1)
                for hh in range(4):
                    r = slice(32 * hh, 32 * hh + 32)
                    mm = pe.matmul(ps[:, 4 + hh, 0:(i + 1) * P], iq[r, i * P:(i + 1) * P], ik[r, 0:(i + 1) * P],
                                   start=True, stop=True)
                mm.then_inc(idx_ready, 1)

            def logits(l, b, u, p, i, w):
                if b == 1 and i >= 1 and u < NT:
                    pe.wait_ge(mask_ready, l * (NT - 1) + i)
                for c in range(2):
                    m = 2 * u + c
                    if m < SRING:
                        pe.wait_ge(acc_free[m], l * (NTILE // RING) + T_ATTENTION[b] // RING)
                    if m >= SRING:
                        pe.wait_ge(exp_ready, l * NM + (b * MAPS + m - SRING + 1))
                    r = slice(HD * c, HD * c + HD)
                    kt = kb[r, 0:w] if b == 1 else k[r, p, 0:w]
                    bank = m % SRING
                    pe.matmul(ps[:, bank, 0:w], q[r, p, i * P:(i + 1) * P], kt, start=True, stop=False)
                    if b == 1 and i >= 1:
                        mm = pe.matmul(ps[:, bank, 0:w], identb[:], maskb[:, WMASK[i - 1]:WMASK[i]], start=False, stop=True)
                    else:
                        mm = pe.matmul(ps[:, bank, i * P:w], identb[:], causalb[:], start=False, stop=True)
                    mm.then_inc(s_ready, 1)

            def gate_steps(l, b, n):
                for step in range(GATE_STEPS[n], GATE_STEPS[n + 1]):
                    m, kk = step // KD, step % KD
                    g = G_GATE[b] + m // 2
                    if kk == 0 and m % 2 == 0:
                        group_wait(l, g)
                    if step == 0:
                        pe.wait_ge(acc_free[GATE_BANK], l * (NTILE // RING) + T_ATTENTION[b] // RING)
                    if kk == 0 and m:
                        pe.wait_ge(gate_free, l * 3 * KD + (b * KD + m))
                    last = product(ps[:, GATE_BANK, :], [(*cols(g % 2, kk, 256, (m % 2) * P, P), kk)], h,
                                   first=kk == 0, final=kk == KD - 1)
                    if kk == KD - 1:
                        last.then_inc(group_done[g % 2] if m % 2 else gate_ready, 1)

            def pt_bank(b, u, c):
                return 4 + (u % 2 if b == 0 else c)

            def transposes(l, b, u, p, i, w):
                n = l * NU + b * UNITS + u
                if b == 0:
                    pe.wait_ge(diff_ready, l * UNITS + u + 1)
                    if u >= 2:
                        pe.wait_ge(pt0_ready, n - 1)
                else:
                    pe.wait_ge(exp_ready, l * NM + (b * MAPS + 2 * u + 2))
                    if u >= 1:
                        pe.wait_ge(pt0_ready, n)
                        pe.wait_ge(pt1_ready, l * NBC + (b - 1) * UNITS + u)
                for c in range(1 if b == 0 else 2):
                    for kb_ in range(i + 1):
                        mm = pe.transpose(ps[:, pt_bank(b, u, c), kb_ * P:(kb_ + 1) * P],
                                          prob[u % 2][:, c, kb_ * P:(kb_ + 1) * P], ident[:])
                mm.then_inc(t_ready, 1)

            def values(l, b, u, p, i, w):
                n = l * NU + b * UNITS + u
                pe.wait_ge(pt0_ready, n + 1)
                if b:
                    pe.wait_ge(pt1_ready, l * NBC + (b - 1) * UNITS + u + 1)
                if u >= 2:
                    pe.wait_ge(ytok_ready, n - 1)
                for c in range(1 if b == 0 else 2):
                    for j in range(i + 1):
                        vals = (v[:, j, p * P:(p + 1) * P], bvw[:, j, 0:HD], v[:, j, p * P + c * HD:p * P + (c + 1) * HD])[b]
                        dst = ps[:, 6 + u % 2, 0:P] if b == 0 else ps[:, 6 + u % 2, c * HD:(c + 1) * HD]
                        mm = pe.matmul(dst, pt[u % 2][:, c, j, :], vals, start=(j == 0), stop=(j == i))
                mm.then_inc(o_ready, 1)

            def attention(l, b):
                pe.wait_ge(rope_ready, l * NROPE + ROPE_AT[b])
                every = list(units())
                for n in range(ITERATIONS):
                    if n < UNITS:
                        logits(l, b, *every[n])
                    gate_steps(l, b, n)
                    if 0 <= n - 1 < UNITS:
                        transposes(l, b, *every[n - 1])
                    if 0 <= n - 2:
                        values(l, b, *every[n - 2])

            def to_features(l, b, pairs):
                for p in pairs:
                    if b == 0:
                        pe.wait_ge(ynorm_ready, l * NPAIR + p + 1)
                    else:
                        pe.wait_ge(ytok_ready, l * NU + b * UNITS + (p + 1) * NT)
                    if p >= 2:
                        pe.wait_ge(y_split, l * 3 * NPAIR + b * NPAIR + p - 1)
                    for i in range(NT):
                        mm = pe.transpose(ps[:, 4 + p % 2, i * P:(i + 1) * P], ytok[:, p * NT + i, :], ident[:])
                    mm.then_inc(yt_ready, 1)

            def branch_product(l, b):
                pe.wait_ge(y_split, l * 3 * NPAIR + (b + 1) * NPAIR)
                for half in range(2):
                    feature_tiles(l, G_BRANCH[b] + half, T_BRANCH[b] + 4 * half, n=4, nk=KW, width=512, rhs=y)

            def shared_values(l):
                pe.wait_ge(acc_free[(T_MISC + 3) % RING], l * (NTILE // RING) + 1)
                for i in range(NT):
                    mm = pe.transpose(ps[:, 5, i * P:(i + 1) * P], bvf[:, i * P:(i + 1) * P], ident[:])
                mm.then_inc(bvt_ready, 1)

            def projections(l, b):
                g, t = G_QKV[b], T_QKV[b]
                feature_tiles(l, g, t, before_tile=None if b else (lambda i: shared_values(l) if i else None))
                if b == 0:
                    pe.wait_ge(bvw_ready, l + 1)
                    indexer(l, 1)
                feature_tiles(l, g + 1, t + 2, before_tile=(lambda i: to_features(l, b - 1, (2 * i, 2 * i + 1))) if b else None)
                if b != 1:
                    if b == 0:
                        indexer(l, 2)
                    feature_tiles(l, g + 2, t + 4)
                    if b == 0:
                        indexer(l, 3)
                    feature_tiles(l, g + 3, t + 6)
                    token_tiles(l, g + 4, t + 8, 2, 2, 256)
                    token_tiles(l, g + 5, t + 10, 2, 2, 256)

            with pe.Fori(0, DEPTH) as l:
                group_wait(l, G_MISC)
                two_tiles_as_ready(G_MISC % 2, (T_MISC, T_MISC + 1), h_ready, l * 2 * KD, h, acc_ready,
                                   lambda c: token_sums(l, 0) if c == KD - 1 else None)
                group_wait(l, G_MISC + 1)
                terms = [(*cols((G_MISC + 1) % 2, kk, 256, 0, P), kk) for kk in range(KD)]
                product(ps[:, T_MISC + 2, :], terms[:KD // 2], h, final=False)
                spread_inverse(l, 0)
                product(ps[:, T_MISC + 2, :], terms[KD // 2:], h, first=False).then_inc(group_done[(G_MISC + 1) % 2], 1)
                feature_tiles(l, G_MISC + 2, T_MISC + 3, n=1)
                projections(l, 0)
                for b in range(3):
                    attention(l, b)
                    pe.wait_ge(gate_free, l * 3 * KD + (b + 1) * KD)
                    if b < 2:
                        projections(l, b + 1)
                    else:
                        to_features(l, b, range(NPAIR))
                    branch_product(l, b)
                for g in range(4):
                    if g < 2:
                        for bank in (2 * g, 2 * g + 1):
                            pe.wait_ge(acc_free[bank], l * (NTILE // RING) + T_FIN // RING)
                    group_wait(l, G_OUT + g)
                    s = (G_OUT + g) % 2
                    if g == 0:
                        two_tiles_as_ready(s, (0, 1), m_split, l * KD, m_, y_ready)
                        continue
                    for i in range(2):
                        last = product(ps[:, 2 * g + i, :], [(*cols(s, kk, 256, i * P, P), kk) for kk in range(KD)], m_)
                        last.then_inc(group_done[s] if i else y_ready, 1)
                statistic(l, 1)
                def swiglu_in(i, j, between=None):
                    s = (G_FIN + i) % 2
                    pe.wait_ge(w_ready[s], l * (NG // 2) + j + ((G_FIN + i) // 2 + 1))
                    for a in range(2):
                        pe.wait_ge(acc_free[2 * i + a], l * (NTILE // RING) + j + T_FIN // RING)
                    two_tiles_as_ready(s, (2 * i, 2 * i + 1), h_ready, l * 2 * KD + KD, h, acc_ready, between)

                def norm_between(c):
                    if c == 4:
                        token_sums(l, 2)
                    if c == 6:
                        spread_inverse(l, 2)

                swiglu_in(0, 0)
                swiglu_in(1, 0, norm_between)
                with pe.Fori(1, KF // 2) as j:
                    for i in range(2):
                        swiglu_in(i, j)
                def ffn_out(s, rhs, first, final):
                    order = [*range(RING, KD), *range(RING)] if first else range(KD)
                    for m in order:
                        if first and m < RING:
                            pe.wait_ge(acc_free[m], l * (NTILE // RING) + NTILE // RING)
                        for kk in range(2):
                            wh, wl = cols(s, kk, D, m * P, P)
                            ah, al = rhs(kk)
                            pe.matmul(ps[:, m, :], wh, ah, start=(first and kk == 0), stop=False, skip_group_check=True)
                            pe.matmul(ps[:, m, :], wh, al, start=False, stop=False, skip_group_check=True)
                            last = pe.matmul(ps[:, m, :], wl, ah, start=False, stop=(final and kk == 1), skip_group_check=True)
                        if m == order[-1]:
                            last.then_inc(group_done[s], 1)
                        elif final:
                            last.then_inc(y_ready, 1)

                def act_static(k0):
                    return lambda kk: (ahi[:, k0 + kk, :], alo[:, k0 + kk, :])

                group_wait(l, G_FOUT)
                pe.wait_ge(act_split, l * KF + 2)
                ffn_out(G_FOUT % 2, act_static(0), True, False)
                with pe.Fori(0, 4) as j:
                    for i in range(2):
                        g = G_FOUT + 1 + i
                        if i == 0:
                            pe.wait_ge(act_split, l * KF + KF)
                        pe.wait_ge(w_ready[g % 2], l * (NG // 2) + j + (g // 2 + 1))
                        ffn_out(g % 2, lambda kk: tuple(a[:, bass.ds(j * 4 + (2 + 2 * i + kk), 1), :].rearrange("p a n -> p (a n)")
                                                        for a in (ahi, alo)), False, False)
                for i in range(2):
                    g = G_FOUT + 9 + i
                    group_wait(l, g)
                    ffn_out(g % 2, act_static(KF - 4 + 2 * i), False, i == 1)
                statistic(l, 3)

        @block.scalar
        def _(act):
            act.wait_ge(consts_made, 11)
            act.wait_ge(lam_dots_ready, 1)
            act.activation(lam_s[:], lam_s[:], ACT.Exp).then_inc(prelude_exp, 1)
            for i, (signed_angle, cos, sin) in enumerate(((res[0], cos64, sin64), (res[1], cos32, sin32))):
                act.wait_ge(angle_ready, 2 * i + 1)
                act.activation(sin[:], signed_angle[:], ACT.Sin).then_inc(sin_done, 1)
                act.wait_ge(angle_ready, 2 * i + 2)
                act.activation(cos[:], cos[:], ACT.Sin, scale=-1.0, bias=half_pi[:]).then_inc(sin_done, 1)

            def square(l, n, c, src):
                if c >= 3:
                    act.wait_ge(sum_ready, l * 4 * NSUM + n * NSUM + c - 2)
                act.activation(tmp[c % 3][:], src, ACT.Square).then_inc(sq_ready, 1)

            def load_sqrt():
                act.activation(unused[:, 0:1], eps[:], ACT.Sqrt)

            def deviation(l, n):
                act.wait_ge(stat_ready, l * 4 + n + 1)
                act.activation(dev[:], ps[:, STAT_BANK[n % 2], 0:NT], ACT.Sqrt, scale=1.0 / D, bias=eps[:]).then_inc(std_ready, 1)

            def residual_norm(l, n):
                weights = g_cur if n else g0
                for c in range(KD):
                    act.wait_ge(x_ready, l * 2 * KD + (X0 + (n // 2) * KD - KD + c + 1))
                    if n == 0:
                        act.wait_ge(g0_ready, l + 1)
                    if n == 0 and c in (0, 4):
                        round_weights(l, G_MISC + c // 4)
                    act.activation(hhi[:, c, :], x[:, c, :], ACT.Copy, scale=weights[:, n * KD + c:n * KD + c + 1]).then_inc(hhi_ready, 1)
                    square(l, n, c, x[:, c, :])
                    if n and c == 2:
                        round_weights(l, G_FIN + 1)
                if n:
                    round_weights(l, G_FIN + 2)
                else:
                    act.drain()
                    load_sqrt()
                deviation(l, n)

            def result_norm(l, n):
                act.drain()
                load_sqrt()
                for m in range(KD):
                    if n == 1 and m % 2 == 0 and m:
                        round_weights(l, G_OUT + m // 2 + 1)
                    how, count = Y_DONE[n // 2][m]
                    if how == "group":
                        act.wait_ge(group_done[count % 2], l * (NG // 2) + count // 2 + 1)
                    else:
                        act.wait_ge(y_ready, l * NY + count)
                    square(l, n, m, ps[:, m, :])
                deviation(l, n)

            def tile_wait(l, t):
                how, count = TILE_DONE[t]
                if how == "group":
                    act.wait_ge(group_done[count % 2], l * (NG // 2) + count // 2 + 1)
                else:
                    act.wait_ge(acc_ready, l * NACC + count)

            def round_weights(l, g):
                s, n = g % 2, g // 2
                act.wait_ge(raw_full[s], (l * (NG // 2) + (n + 1)) * 16)
                if n:
                    act.wait_ge(group_done[s], l * (NG // 2) + n)
                act.activation(whi[s][:], raw[s][:], ACT.Copy).then_inc(whi_ready[s], 1)

            def exponentials(l, b, u, p, i, w):
                n = l * NU + b * UNITS + u
                for c in range(2):
                    act.wait_ge(max_ready, l * NM + (b * MAPS + 2 * u + c + 1))
                    if u >= 2:
                        act.wait_ge(t_ready, n - 1)
                    act.activation(prob[u % 2][:, c, 0:w], ps[:, (2 * u + c) % SRING, 0:w], ACT.Exp,
                                   bias=negmax[:, u, c:c + 1], accum_out=esum[:, u, c:c + 1]).then_inc(exp_ready, 1)

            def keep_gate(l, m):
                gate_wait(act, l, 0, m)
                act.activation(gate[:, m, :], ps[:, GATE_BANK, :], ACT.Copy).then_inc(gate_free, 1)

            def copy_transposed(l, b, u, p, i, w):
                n = l * NU + b * UNITS + u
                act.wait_ge(t_ready, n + 1)
                if u >= 2:
                    act.wait_ge(o_ready, n - 1)
                bank = 4 + (u % 2 if b == 0 else 0)
                act.activation(pt[u % 2][:, 0, 0:i + 1, :], ps[:, bank, 0:w].rearrange("p (k q) -> p k q", q=P),
                               ACT.Copy).then_inc(pt0_ready, 1)

            def values(l, b):
                g, t = G_QKV[b], T_QKV[b]
                round_weights(l, g + 4)
                round_weights(l, g + 5)
                for n in range(4):
                    tile_wait(l, t + 8 + n)
                    vg, hf = n // 2, n % 2
                    for i in range(2):
                        copy = act.activation(v[:, 2 * hf + i, vg * 256:(vg + 1) * 256], ps[:, (t + n) % RING, i * 256:(i + 1) * 256],
                                              ACT.Copy, scale=inv[:, 2 * hf + i:2 * hf + i + 1])
                    copy.then_inc(acc_free[(t + n) % RING], 1)
                    if hf:
                        round_weights(l, g + 6 + vg)

            def high_results(l, b, pairs):
                for p in pairs:
                    act.wait_ge(yt_ready, l * 3 * NPAIR + b * NPAIR + p + 1)
                    act.activation(yhi[:, p, :], ps[:, 4 + p % 2, :], ACT.Copy).then_inc(yhi_ready, 1)

            with act.Fori(0, DEPTH) as l:
                residual_norm(l, 0)
                round_weights(l, 2)
                round_weights(l, 3)
                tile_wait(l, T_MISC + 3)
                act.activation(bvf[:], ps[:, (T_MISC + 3) % RING, :], ACT.Copy).then_inc(acc_free[(T_MISC + 3) % RING], 1)
                round_weights(l, 4)
                act.wait_ge(bvt_ready, l + 1)
                act.wait_ge(inv_ready, l * 4 + 1)
                for i in range(NT):
                    copy = act.activation(bvw[:, i, :], ps[:, 5, i * P:(i + 1) * P], ACT.Copy, scale=inv[:, i:i + 1])
                copy.then_inc(bvw_ready, 1)
                round_weights(l, G_QKV[0] + 2)
                round_weights(l, G_QKV[0] + 3)
                values(l, 0)
                for b in range(3):
                    g = G_GATE[b] + 6
                    every = list(units())
                    for n in range(UNITS + 3):
                        if n < UNITS:
                            exponentials(l, b, *every[n])
                        for m in range(KD):
                            if b == 0 and n < ITERATIONS and completes(n, m):
                                keep_gate(l, m)
                        if 0 <= n - 1 < UNITS:
                            copy_transposed(l, b, *every[n - 1])
                        for m in range(1, KD, 2):
                            if n < ITERATIONS and completes(n, m):
                                round_weights(l, G_GATE[b] + m // 2 + 2)
                        if b == 0 and n >= 3:
                            u = n - 3
                            if u:
                                act.wait_ge(ysq_ready, l * UNITS + u)
                            act.wait_ge(o_ready, l * NU + u + 1)
                            o = ps[:, 6 + u % 2, 0:P]
                            act.activation(unused[:], o, ACT.Square, scale=rinv[:, u, 0:1], accum_out=ysq[:, u:u + 1]).then_inc(ysq_ready, 1)
                            act.activation(ytok[:, u, :], o, ACT.Copy, scale=rinv[:, u, 0:1]).then_inc(ytok_ready, 1)
                    if b == 0:
                        act.wait_ge(ysq_ready, l * UNITS + UNITS)
                        act.activation(ystd[:], ysq[:], ACT.Sqrt, scale=1.0 / (2 * HD), bias=eps[:]).then_inc(ystd_ready, 1)
                    high_results(l, b, (0, 1))
                    if b < 2:
                        round_weights(l, g)
                    high_results(l, b, (2, 3))
                    for m in range(KD):
                        if b == 0:
                            act.wait_ge(gate_rs_ready, l * KD + m + 1)
                        elif m == 0:
                            act.wait_ge(gate_free, l * 3 * KD + (b + 1) * KD)
                        act.activation(gate[:, m, :], gate[:, m, :], ACT.Sigmoid).then_inc(sig_ready, 1)
                    if b < 2:
                        round_weights(l, g + 1)
                    if b == 1:
                        values(l, 2)
                    round_weights(l, G_BRANCH[b] + 2)
                    round_weights(l, G_BRANCH[b] + 3)
                result_norm(l, 1)
                residual_norm(l, 2)
                with act.Fori(0, KF // 2) as j:
                    for i in range(2):
                        act.wait_ge(gate_scaled, l * KF + j * 2 + (i + 1))
                        act.activation(tmp[i][:], tmp[i][:], ACT.Silu).then_inc(silu_ready, 1)
                        s, n = (G_FIN + i + 1) % 2, (G_FIN + i + 3) // 2
                        act.wait_ge(raw_full[s], (l * (NG // 2) + j + (n + 1)) * 16)
                        act.wait_ge(group_done[s], l * (NG // 2) + j + n)
                        act.activation(whi[s][:], raw[s][:], ACT.Copy).then_inc(whi_ready[s], 1)
                for g in range(G_FOUT + 3, NG):
                    round_weights(l, g)
                result_norm(l, 3)

        @block.vector
        def _(dve):
            parts = two_pi_parts()
            dve.wait_ge(lam_loaded, 16)
            lam4 = lam_v[:].rearrange("p (l v) d -> p l v d", v=4)
            lam_q, lam_k = lam4[:, :, 0:2, :], lam4[:, :, 2:4, :]
            lam_p = tmp[0][:, 0:DEPTH * 2 * HD].rearrange("p (l v d) -> p l v d", l=DEPTH, v=2)
            dve.tensor_tensor(lam_p, lam_q, lam_k, ALU.mult)
            dve.drain()
            dve.tensor_reduce(lam_s[:], lam_p, axis=X, op=ALU.add).then_inc(lam_dots_ready, 1)
            dve.wait_ge(angle_loaded, 16 * 2)
            angle, turns = res
            dve.tensor_copy(turns[:], y0[:].bitcast(i32))
            dve.drain()
            dve.tensor_scalar(angle[:], turns[:], const[:, C_INV:C_INV + 1], None, ALU.mult)
            dve.drain()
            magic = 1.5 * 2 ** 23
            dve.tensor_scalar(turns[:], angle[:], 1 / (2 * math.pi), magic, ALU.mult, ALU.add)
            dve.drain()
            dve.tensor_scalar(turns[:], turns[:], magic, None, ALU.subtract)
            dve.drain()
            for part in parts:
                dve.scalar_tensor_tensor(angle[:], turns[:], -part, angle[:], ALU.mult, ALU.add)
                dve.drain()
            dve.tensor_scalar(angle[:], angle[:], -3.1415925, 3.1415925, ALU.max, ALU.min)
            dve.drain()
            dve.stream_shuffle(turns[:], angle[:], [*range(16, 24), *range(8, 16), *range(8), *range(24, 32)])
            for a, cos, sgn in ((angle, cos64, C_SGN64), (turns, cos32, C_SGN32)):
                dve.drain()
                dve.tensor_scalar(a[:], a[:], const[:, sgn:sgn + 1], None, ALU.mult).then_inc(angle_ready, 1)
                dve.drain()
                dve.scalar_tensor_tensor(cos[:], a[:], -1.0, a[:], ALU.mult, ALU.max).then_inc(angle_ready, 1)
            dve.wait_ge(small_loaded, 16 * 2)
            dve.wait_ge(prelude_exp, 1)
            for layer in range(DEPTH):
                dve.tensor_tensor(neglam_all[:, layer:layer + 1], lam_s[:, layer, 1:2], lam_s[:, layer, 0:1], ALU.subtract)
                dve.drain()
                dve.tensor_scalar(neglam_all[:, layer:layer + 1], neglam_all[:, layer:layer + 1], lam_init(layer), None, ALU.subtract)
                dve.tensor_scalar(subg_all[:, layer, :], subg_all[:, layer, :], 1.0 - lam_init(layer), None, ALU.mult)
            dve.tensor_copy(g0[:], g_all[:, 0, 0:KD]).then_inc(g0_ready, 1)
            dve.wait_ge(sin_done, 4)

            swap = {n: [*range(n // 8, n // 4), *range(n // 8), *range(n // 4, 32)] for n in (64, 32)}

            def tile_wait(l, t):
                dve.drain()
                how, count = TILE_DONE[t]
                if how == "group":
                    dve.wait_ge(group_done[count % 2], l * (NG // 2) + count // 2 + 1)
                else:
                    dve.wait_ge(acc_ready, l * NACC + count)

            def rotate(l, t, dst, cos, sin, mask, scale=1.0):
                src = ps[:, t % RING, :]
                dve.drain()
                tile_wait(l, t)
                dve.scalar_tensor_tensor(tmp[2][:], src, scale, cos[:], ALU.mult, ALU.mult)
                dve.stream_shuffle(tmp[1][:], src, mask).then_inc(acc_free[t % RING], 1)
                dve.drain()
                dve.scalar_tensor_tensor(tmp[1][:], tmp[1][:], scale, sin[:], ALU.mult, ALU.mult)
                dve.drain()
                dve.tensor_tensor(dst, tmp[1][:], tmp[2][:], ALU.add).then_inc(rope_ready, 1)

            def inverse_deviation(l, n):
                dve.drain()
                dve.wait_ge(std_ready, l * 4 + n + 1)
                dve.reciprocal(inv[:], dev[:]).then_inc(inv_ready, 1)

            def low_input(l, n, c):
                weights = g_cur if n else g0
                dve.wait_ge(hhi_ready, l * 2 * KD + ((n // 2) * KD + c + 1))
                dve.scalar_tensor_tensor(hlo[:, c, :], x[:, c, :], weights[:, n * KD + c:n * KD + c + 1], hhi[:, c, :].bitcast(f32),
                                         ALU.mult, ALU.subtract).then_inc(h_ready, 1)

            def residual_inverse(l, n):
                inverse_deviation(l, n)
                dve.wait_ge(rs_ready, l * 4 + n + 1)
                dve.tensor_copy(rs_h[:], ps[:, STAT_BANK[0], :])
                dve.drain()

            def result_norm(l, n):
                dve.drain()
                dve.wait_ge(sq_ready, l * 4 * KD + n * KD + 1)
                dve.tensor_copy(y0[:], ps[:, 0, :]).then_inc(y0_copied, 1)
                for c in range(1, KD):
                    dve.drain()
                    add_squares(dve, l, n, c)
                inverse_deviation(l, n)
                dve.wait_ge(rs_ready, l * 4 + n + 1)
                dve.tensor_copy(rs_res[:], ps[:, STAT_BANK[1], :])
                dve.drain()
                at_ = l * 2 * KD + (n // 2) * KD
                bufs = (*res, y0)
                for c in range(KD + 1):
                    if c < KD:
                        if c >= 3:
                            dve.wait_ge(x_ready, at_ + (X0 + c - 2))
                        src = y0[:] if c == 0 else ps[:, c, :]
                        dve.scalar_tensor_tensor(bufs[c % 3][:], src, g_cur[:, n * KD + c:n * KD + c + 1], rs_res[:],
                                                 ALU.mult, ALU.mult).then_inc(res_ready, 1)
                    if c >= 1:
                        dve.wait_ge(res_ready, at_ + c)
                        dve.tensor_tensor(x[:, c - 1, :], x[:, c - 1, :], bufs[(c - 1) % 3][:], ALU.add).then_inc(x_ready, 1)
                    if n == 1 and c >= 2:
                        low_input(l, 2, c - 2)
                if n == 1:
                    low_input(l, 2, KD - 1)

            def index_scores(l, i):
                w = (i + 1) * P
                score, term = scores[:, WMASK[i - 1]:WMASK[i]], tmp[0][:, 0:w]
                dve.drain()
                dve.wait_ge(idx_ready, l * (NT - 1) + i)
                if i == 1:
                    dve.wait_ge(bvw_ready, l + 1)
                for hh in range(4):
                    op = dve.tensor_scalar(term if hh else score, ps[:, 4 + hh, 0:w], 0.0, bvw[:, i, HD + hh:HD + hh + 1],
                                           ALU.max, ALU.mult)
                    if hh == 3:
                        op.then_inc(idx_used, 1)
                    dve.drain()
                    if hh:
                        dve.tensor_tensor(score, score, term, ALU.add)
                        dve.drain()
                past = scores[:, WMASK[i] - P:WMASK[i]]
                dve.tensor_tensor(past, past, causal[:], ALU.add)

            def top_k_rounds(first, n):
                tiles = [scores[:, WMASK[i - 1]:WMASK[i]] for i in range(1, NT)]
                for r in range(first, first + n):
                    dve.drain()
                    for i, score in enumerate(tiles):
                        dve.max(out=top8[:, 8 * i:8 * i + 8], in_=score)
                    dve.drain()
                    for i, score in enumerate(tiles):
                        dve.match_replace(out=score, in_to_replace=top8[:, 8 * i:8 * i + 8], in_values=score, imm_value=TAKEN)
                    if r == ROUNDS - 1:
                        dve.drain()
                        for i, score in enumerate(tiles):
                            dve.tensor_scalar(maskb[:, WMASK[i]:WMASK[i + 1]], score, TAKEN / 2, -BIG, ALU.is_gt, ALU.mult)\
                               .then_inc(mask_ready, 1)

            def maxima(l, b, u, p, i, w):
                for c in range(2):
                    m = 2 * u + c
                    dve.wait_ge(s_ready, l * NM + (b * MAPS + m + 1))
                    dve.tensor_reduce(negmax[:, u, c:c + 1], ps[:, m % SRING, 0:w], axis=X, op=ALU.max, negate=True)\
                       .then_inc(max_ready, 1)

            def after_exp(l, b, u, p, i, w):
                dve.wait_ge(exp_ready, l * NM + (b * MAPS + 2 * u + 2))
                dve.reciprocal(rinv[:, u, :], esum[:, u, :])
                if b == 0:
                    pr = prob[u % 2]
                    dve.drain()
                    dve.scalar_tensor_tensor(ratio[:], esum[:, u, 0:1], rinv[:, u, 1:2], neglam[:], ALU.mult, ALU.mult)
                    dve.drain()
                    dve.scalar_tensor_tensor(pr[:, 0, 0:w], pr[:, 1, 0:w], ratio[:], pr[:, 0, 0:w],
                                             ALU.mult, ALU.add).then_inc(diff_ready, 1)

            def scale_gates(l, tiles):
                for m in tiles:
                    dve.wait_ge(gate_free, l * 3 * KD + m + 1)
                    dve.tensor_tensor(gate[:, m, :], gate[:, m, :], rs_h[:], ALU.mult).then_inc(gate_rs_ready, 1)

            def copy_transposed(l, b, u, p, i, w):
                n = l * NU + b * UNITS + u
                dve.wait_ge(t_ready, n + 1)
                if u >= 2:
                    dve.wait_ge(o_ready, n - 1)
                dve.tensor_copy(pt[u % 2][:, 1, 0:i + 1, :], ps[:, 5, 0:w].rearrange("p (k q) -> p k q", q=P)).then_inc(pt1_ready, 1)

            def results(l, b, u, p, i, w):
                dve.wait_ge(o_ready, l * NU + b * UNITS + u + 1)
                o = ps[:, 6 + u % 2, :]
                for c in range(2):
                    op = dve.tensor_scalar(ytok[:, u, c * HD:(c + 1) * HD], o[:, c * HD:(c + 1) * HD],
                                           rinv[:, u, c:c + 1], None, ALU.mult)
                op.then_inc(ytok_ready, 1)

            def low_results(l, b, pairs):
                for p in pairs:
                    dve.wait_ge(yhi_ready, l * 3 * NPAIR + b * NPAIR + p + 1)
                    dve.tensor_tensor(ylo[:, p, :], ps[:, 4 + p % 2, :], yhi[:, p, :].bitcast(f32), ALU.subtract).then_inc(y_split, 1)

            def projections(l, b):
                for i in range(4):
                    rotate(l, T_QKV[b] + i, q[:, i, :], cos64r, sin64r, swap[64], SCALE)
                    if b and i in (1, 2):
                        low_results(l, b - 1, (2 * i - 2, 2 * i - 1))
                    if b == 0 and i in (1, 3):
                        index_scores(l, (i + 1) // 2)
                if b != 1:
                    for i in range(4):
                        rotate(l, T_QKV[b] + 4 + i, k[:, i, :], cos64r, sin64r, swap[64])
                        if b == 0 and i == 1:
                            index_scores(l, 3)

            with dve.Fori(0, DEPTH) as l:
                dve.drain()
                dve.tensor_copy(g_cur[:], g_all[:, bass.ds(l, 1), :].rearrange("p a n -> p (a n)"))
                dve.tensor_copy(subg[:], subg_all[:, bass.ds(l, 1), :].rearrange("p a n -> p (a n)"))
                dve.tensor_copy(neglam[:], neglam_all[:, bass.ds(l, 1)])
                dve.drain()
                for c in range(KD):
                    low_input(l, 0, c)
                residual_inverse(l, 0)
                dve.tensor_tensor(cos64r[:], cos64[:], rs_h[:], ALU.mult)
                dve.tensor_tensor(sin64r[:], sin64[:], rs_h[:], ALU.mult)
                rotate(l, T_MISC, kb[:], cos64r, sin64r, swap[64])
                dve.tensor_tensor(cos32r[:], cos32[:], rs_h[:], ALU.mult)
                dve.tensor_tensor(sin32r[:], sin32[:], rs_h[:], ALU.mult)
                rotate(l, T_MISC + 1, ik[:], cos32r, sin32r, swap[32])
                rotate(l, T_MISC + 2, iq[:], cos32r, sin32r, swap[32])
                projections(l, 0)
                top_k_rounds(0, ROUNDS - len(TOPK_AT))
                for b in range(3):
                    every = list(units())
                    for n in range(ITERATIONS):
                        if 1 <= n <= UNITS:
                            after_exp(l, b, *every[n - 1])
                        if n < UNITS:
                            maxima(l, b, *every[n])
                        if b == 0 and n in TOPK_AT:
                            top_k_rounds(ROUNDS - len(TOPK_AT) + TOPK_AT.index(n), 1)
                        if b == 0 and 14 <= n < 17:
                            scale_gates(l, (2 * (n - 14), 2 * (n - 14) + 1))
                        for m in range(KD):
                            if b and completes(n, m):
                                gate_wait(dve, l, b, m)
                                dve.tensor_tensor(gate[:, m, :], ps[:, GATE_BANK, :], rs_h[:], ALU.mult).then_inc(gate_free, 1)
                        if b and 0 <= n - 1 < UNITS:
                            copy_transposed(l, b, *every[n - 1])
                        if b and n >= 2:
                            results(l, b, *every[n - 2])
                    if b == 0:
                        scale_gates(l, (KD - 2, KD - 1))
                        dve.wait_ge(ystd_ready, l + 1)
                        dve.reciprocal(yrs[:], ystd[:])
                        dve.drain()
                        for u, p, i, w in units():
                            op = dve.scalar_tensor_tensor(ytok[:, u, :], ytok[:, u, :], yrs[:, u:u + 1], subg[:], ALU.mult, ALU.mult)
                            if i == NT - 1:
                                op.then_inc(ynorm_ready, 1)
                    if b < 2:
                        projections(l, b + 1)
                    else:
                        low_results(l, b, range(NPAIR))
                    for m in range(KD):
                        t = T_BRANCH[b] + m
                        tile_wait(l, t)
                        dve.wait_ge(sig_ready, l * 3 * KD + (b * KD + m + 1))
                        dst = merged[:, m, :] if b == 0 else tmp[1][:]
                        dve.tensor_tensor(dst, ps[:, t % RING, :], gate[:, m, :], ALU.mult)\
                           .then_inc(acc_free[t % RING], 1)
                        if b:
                            dve.drain()
                            dve.tensor_tensor(merged[:, m, :], merged[:, m, :], tmp[1][:], ALU.add)
                        if b == 2:
                            dve.drain()
                            dve.tensor_copy(mhi[:, m, :], merged[:, m, :])
                            dve.drain()
                            dve.tensor_tensor(mlo[:, m, :], merged[:, m, :], mhi[:, m, :].bitcast(f32), ALU.subtract).then_inc(m_split, 1)
                result_norm(l, 1)
                residual_inverse(l, 2)
                dve.tensor_copy(g0[:], g_cur[:, 4 * KD:]).then_inc(g0_ready, 1)
                with dve.Fori(0, KF // 2) as j:
                    for i in range(2):
                        dve.drain()
                        dve.wait_ge(acc_ready, l * NACC + j * 2 + (ACC_FIN + i))
                        dve.tensor_tensor(tmp[i][:], ps[:, 2 * i, :], rs_h[:], ALU.mult).then_inc(gate_scaled, 1)
                        dve.wait_ge(group_done[(G_FIN + i) % 2], l * (NG // 2) + j + ((G_FIN + i) // 2 + 1))
                        dve.wait_ge(gate_scaled, l * KF + j * 2 + (i + 1))
                        dve.tensor_tensor(tmp[2][:], ps[:, 2 * i + 1, :], rs_h[:], ALU.mult).then_inc(acc_free[2 * i + 1], 1)
                        dve.drain()
                        dve.wait_ge(silu_ready, l * KF + j * 2 + (i + 1))
                        f = bass.ds(j * 2 + i, 1)
                        ah, al = (a[:, f, :].rearrange("p a n -> p (a n)") for a in (ahi, alo))
                        dve.tensor_tensor(tmp[2][:], tmp[i][:], tmp[2][:], ALU.mult).then_inc(acc_free[2 * i], 1)
                        dve.drain()
                        dve.tensor_copy(ah, tmp[2][:])
                        dve.drain()
                        dve.tensor_tensor(al, tmp[2][:], ah.bitcast(f32), ALU.subtract).then_inc(act_split, 1)
                result_norm(l, 3)


def groups(a, width):
    kk = GCOLS // width
    kdim, n = a.shape
    a = a.reshape(kdim // (P * kk), kk, P, n // width, width)
    return a.transpose(3, 0, 2, 1, 4).reshape(-1, P, GCOLS)


def weight_stream(w_in, w_branch, w_out, w_ffn_in, w_ffn_out):
    stream = []
    for layer in range(DEPTH):
        w = w_in[layer]
        cut = np.cumsum([0, 512, 512, 512, 512, HD, HD, 128, 32, 4, 512, 512, 512])
        aq, ak, av, bq, bk, bv, iq, ik, iw, cq, ck, cv = (w[:, cut[i]:cut[i] + n] for i, n in enumerate(
            (512, 512, 512, 512, HD, HD, 128, 32, 4, 512, 512, 512)))
        misc = [bk, bk, ik, ik, ik, ik, iq, iq] + ([bv] + [iw] * 16) * 2
        stream.append(groups(np.concatenate(misc, axis=1), 256))
        qkv = ([aq, ak, av], [bq], [cq, ck, cv])
        stream.append(groups(np.concatenate(qkv[0], axis=1), 256))
        for b in range(3):
            stream.append(groups(w[:, cut[-1] + b * D:cut[-1] + (b + 1) * D], 256))
            if b < 2:
                stream.append(groups(np.concatenate(qkv[b + 1], axis=1), 256))
            stream.append(groups(w_branch[layer, b], 512))
        stream.append(groups(w_out[layer], 256))
        fin = w_ffn_in[layer].reshape(D, 2, KF, P).transpose(0, 2, 1, 3).reshape(D, 2 * FF)
        stream += [groups(fin, 256), groups(w_ffn_out[layer], D)]
    return np.ascontiguousarray(np.concatenate(stream))


def constants():
    c = np.zeros((P, NCONST), np.float32)
    for n, sgn, first in ((64, C_SGN64, 0), (32, C_SGN32, 16)):
        rot = n // 4
        freq = np.power(np.float32(500000.0), -np.arange(rot // 2, dtype=np.float32) * np.float32(2.0) / np.float32(rot))
        for p in range(P):
            if first <= p % 32 < first + rot:
                c[p, C_INV] = freq[(p % 32 - first) % (rot // 2)]
            if p % n < rot:
                c[p, sgn] = -1.0 if p % n < rot // 2 else 1.0
    return c


def kernel(x, positions, w_in, w_branch, w_out, lambda_q1, lambda_k1, lambda_q2, lambda_k2, subln_g, norm_g,
           w_ffn_in, w_ffn_out):
    import concourse.bacc as bacc
    from concourse.bass_utils import run_bass_kernel_spmd

    x, w_in, w_branch, w_out, w_ffn_in, w_ffn_out = map(np.asarray, (x, w_in, w_branch, w_out, w_ffn_in, w_ffn_out))
    lam = np.stack([np.asarray(a) for a in (lambda_q1, lambda_q2, lambda_k1, lambda_k2)], axis=1)
    g = np.asarray(norm_g).reshape(DEPTH, 4 * KD, P)
    arrays = {
        "x_in": np.ascontiguousarray(x[0].T.reshape(KD, P, SEQ).transpose(1, 0, 2)),
        "pos_in": np.ascontiguousarray(np.asarray(positions)),
        "w_in": weight_stream(w_in, w_branch, w_out, w_ffn_in, w_ffn_out),
        "lam_in": np.ascontiguousarray(lam.reshape(1, -1)),
        "subg_in": np.ascontiguousarray(np.asarray(subln_g).reshape(1, -1)),
        "g_in": np.ascontiguousarray(np.concatenate([g, np.roll(g[:, :KD], -1, axis=0)], axis=1).transpose(2, 0, 1)),
        "const_in": constants(),
    }
    nc = bacc.Bacc("TRN2", target_bir_lowering=False, num_devices=1,
                   dynamic_dma_scratch_size=1024)
    args = [nc.dram_tensor(n, a.shape, mybir.dt.from_np(a.dtype), kind="ExternalInput").ap() for n, a in arrays.items()]
    out = nc.dram_tensor("out", (P, KD, SEQ), mybir.dt.float32, kind="ExternalOutput").ap()
    trunk(nc, *args, out)
    r = run_bass_kernel_spmd(nc, [arrays], core_ids=[0])
    got = np.asarray(r.results[0]["out"])
    return np.ascontiguousarray(got.transpose(1, 0, 2).reshape(D, SEQ).T)[None]
```
